# Optimizing a Trainium2 kernel written in Bass

```python
import jax, jax.numpy as jnp
from jax import lax
import numpy as np

D_MODEL = 1024
BATCH = 1
SEQ = 512
DEPTH = 1
DEC_BATCH = 1
DEC_SEQ = 32
PAST_LEN = 512

CHUNK = 64
MIX_WIDTH = D_MODEL
GM_WIDTH = MIX_WIDTH // 2
GM_GROUPS = 4
GM_GROUP_DIM = GM_WIDTH // GM_GROUPS
GM_CHUNK = 128
SB_WIDTH = MIX_WIDTH - GM_WIDTH
SB_HEAD_DIM = 64
SB_HEADS = SB_WIDTH // SB_HEAD_DIM
SB_BLOCK = 128
IN_WIDTH = 2 * GM_WIDTH + 3 * SB_WIDTH
N_EXPERT_GROUPS = 4
EXPERTS_PER_GROUP = 4
N_EXPERTS = N_EXPERT_GROUPS * EXPERTS_PER_GROUP
TOP_K = 2
EXPERT_FF = D_MODEL // 4
EPS = 1e-6

kernel_name = "hybrid_gmlp_stickbreaking_hmoe_stream_step"

def rmsnorm(x, g):
    xf = x.astype(jnp.float32)
    y = xf * lax.rsqrt(jnp.mean(xf * xf, axis=-1, keepdims=True) + EPS)
    return (y * g.astype(jnp.float32)).astype(x.dtype)

def mixer_inputs(xn, w_in, gm_v_norm_g, q_norm_g, k_norm_g):
    b, t, _ = xn.shape
    proj = xn @ w_in
    gm_u, gm_v, q, k, v = jnp.split(
        proj, [GM_WIDTH, 2 * GM_WIDTH, 2 * GM_WIDTH + SB_WIDTH, 2 * GM_WIDTH + 2 * SB_WIDTH], axis=-1)
    gm_u = jax.nn.gelu(gm_u).reshape(b, t, GM_GROUPS, GM_GROUP_DIM)
    gm_v = rmsnorm(jax.nn.gelu(gm_v), gm_v_norm_g).reshape(b, t, GM_GROUPS, GM_GROUP_DIM)
    q = rmsnorm(q.reshape(b, t, SB_HEADS, SB_HEAD_DIM), q_norm_g)
    k = rmsnorm(k.reshape(b, t, SB_HEADS, SB_HEAD_DIM), k_norm_g)
    v = v.reshape(b, t, SB_HEADS, SB_HEAD_DIM)
    return gm_u, gm_v, q, k, v

def gmlp_chunk(u, v, w_s, b_s):
    tc = v.shape[-3]
    mask = jnp.tril(jnp.ones((GM_CHUNK, GM_CHUNK), dtype=bool))
    w = jnp.where(mask, w_s, 0)[:, :tc, :tc]
    mixed = jnp.einsum('gts,...sgd->...tgd', w, v) + b_s[:, :tc].T[:, :, None]
    return u * mixed

def stick_breaking(q, k, v, q_pos, k_pos):
    z = jnp.einsum('bqhd,bshd->bhqs', q, k).astype(jnp.float32) * (SB_HEAD_DIM ** -0.5)
    causal = k_pos[None, :] < q_pos[:, None]
    log_beta = jax.nn.log_sigmoid(z)
    log_keep = jnp.where(causal, log_beta - z, 0.0)
    rest = lax.cumsum(log_keep, axis=3, reverse=True) - log_keep
    w = jnp.where(causal, jnp.exp(log_beta + rest), 0.0)
    return jnp.einsum('bhqs,bshd->bqhd', w.astype(v.dtype), v)

def hier_moe(x, w_router_group, b_router_group, w_router_expert, b_router_expert,
             w_gate, w_up, w_down):
    shp = x.shape
    xf = x.reshape(-1, shp[-1])
    lg = (xf @ w_router_group).astype(jnp.float32) + b_router_group.astype(jnp.float32)
    p_g = jax.nn.softmax(lg, axis=-1)
    g_sel = jnp.argmax(lg, axis=-1)
    p_sel = jnp.take_along_axis(p_g, g_sel[:, None], axis=-1)[:, 0]
    le = jnp.einsum('nd,gde->nge', xf, w_router_expert).astype(jnp.float32) \
        + b_router_expert.astype(jnp.float32)
    le = jnp.take_along_axis(le, g_sel[:, None, None], axis=1)[:, 0]
    p_e = jax.nn.softmax(le, axis=-1)
    top_v, top_i = lax.top_k(p_e, TOP_K)
    gates = p_sel[:, None] * top_v / jnp.sum(top_v, axis=-1, keepdims=True)
    expert_ids = g_sel[:, None] * EXPERTS_PER_GROUP + top_i
    combine = jnp.sum(jax.nn.one_hot(expert_ids, N_EXPERTS, dtype=jnp.float32)
                      * gates[..., None], axis=1).astype(x.dtype)
    hg = jnp.einsum('nd,edf->nef', xf, w_gate)
    hu = jnp.einsum('nd,edf->nef', xf, w_up)
    a = jax.nn.silu(hg) * hu * combine[:, :, None]
    y = jnp.einsum('nef,efd->nd', a, w_down)
    return y.reshape(shp)

def setup_inputs(seed: int = 0) -> dict:
    key = jax.random.key(seed)
    ks = jax.random.split(key, 24)
    f32 = jnp.float32
    nrm = lambda k, s, sc: jax.random.normal(k, s, f32) * sc
    L = DEPTH
    return {
        "x_prompt": nrm(ks[0], (BATCH, SEQ, D_MODEL), 1.0),
        "x_sample": nrm(ks[1], (DEC_BATCH, DEC_SEQ, D_MODEL), 1.0),
        "cache_sb_k": nrm(ks[2], (L, DEC_BATCH, PAST_LEN, SB_HEADS, SB_HEAD_DIM), 1.0),
        "cache_sb_v": nrm(ks[3], (L, DEC_BATCH, PAST_LEN, SB_HEADS, SB_HEAD_DIM), 1.0),
        "norm1_g": 1.0 + nrm(ks[4], (L, D_MODEL), 0.02),
        "w_in": nrm(ks[5], (L, D_MODEL, IN_WIDTH), D_MODEL ** -0.5),
        "gm_v_norm_g": 1.0 + nrm(ks[6], (L, GM_WIDTH), 0.02),
        "gm_w_s": nrm(ks[7], (L, GM_GROUPS, GM_CHUNK, GM_CHUNK), GM_CHUNK ** -0.5),
        "gm_b_s": nrm(ks[8], (L, GM_GROUPS, GM_CHUNK), 0.02),
        "q_norm_g": 1.0 + nrm(ks[9], (L, SB_HEAD_DIM), 0.02),
        "k_norm_g": 1.0 + nrm(ks[10], (L, SB_HEAD_DIM), 0.02),
        "w_out": nrm(ks[11], (L, MIX_WIDTH, D_MODEL), MIX_WIDTH ** -0.5),
        "norm2_g": 1.0 + nrm(ks[12], (L, D_MODEL), 0.02),
        "w_router_group": nrm(ks[13], (L, D_MODEL, N_EXPERT_GROUPS), D_MODEL ** -0.5),
        "b_router_group": nrm(ks[14], (L, N_EXPERT_GROUPS), 0.01),
        "w_router_expert": nrm(ks[15], (L, N_EXPERT_GROUPS, D_MODEL, EXPERTS_PER_GROUP), D_MODEL ** -0.5),
        "b_router_expert": nrm(ks[16], (L, N_EXPERT_GROUPS, EXPERTS_PER_GROUP), 0.01),
        "w_gate": nrm(ks[17], (L, N_EXPERTS, D_MODEL, EXPERT_FF), D_MODEL ** -0.5),
        "w_up": nrm(ks[18], (L, N_EXPERTS, D_MODEL, EXPERT_FF), D_MODEL ** -0.5),
        "w_down": nrm(ks[19], (L, N_EXPERTS, EXPERT_FF, D_MODEL), EXPERT_FF ** -0.5),
    }

def reference(x_prompt, x_sample, cache_sb_k, cache_sb_v, norm1_g, w_in, gm_v_norm_g,
              gm_w_s, gm_b_s, q_norm_g, k_norm_g, w_out, norm2_g, w_router_group,
              b_router_group, w_router_expert, b_router_expert, w_gate, w_up, w_down):
    yp, ys = x_prompt, x_sample
    kp_list, vp_list, ks_list, vs_list, gv_list = [], [], [], [], []
    for l in range(DEPTH):
        moe_args = (w_router_group[l], b_router_group[l], w_router_expert[l],
                    b_router_expert[l], w_gate[l], w_up[l], w_down[l])
        b, s, _ = yp.shape
        xn = rmsnorm(yp, norm1_g[l])
        gu, gv, q, k, v = mixer_inputs(xn, w_in[l], gm_v_norm_g[l], q_norm_g[l], k_norm_g[l])
        nc = s // GM_CHUNK
        gm = gmlp_chunk(gu.reshape(b, nc, GM_CHUNK, GM_GROUPS, GM_GROUP_DIM),
                        gv.reshape(b, nc, GM_CHUNK, GM_GROUPS, GM_GROUP_DIM),
                        gm_w_s[l], gm_b_s[l]).reshape(b, s, GM_WIDTH)
        nb = s // SB_BLOCK
        k_pos = jnp.arange(s, dtype=jnp.int32)
        q_blocks = q.reshape(b, nb, SB_BLOCK, SB_HEADS, SB_HEAD_DIM).transpose(1, 0, 2, 3, 4)
        pos_blocks = k_pos.reshape(nb, SB_BLOCK)
        sb = lax.map(lambda a: stick_breaking(a[0], k, v, a[1], k_pos), (q_blocks, pos_blocks))
        sb = sb.transpose(1, 0, 2, 3, 4).reshape(b, s, SB_WIDTH)
        h = yp + jnp.concatenate([gm, sb], axis=-1) @ w_out[l]
        yp = h + hier_moe(rmsnorm(h, norm2_g[l]), *moe_args)
        kp_list.append(k)
        vp_list.append(v)
        db, n, _ = ys.shape
        xn = rmsnorm(ys, norm1_g[l])
        gu, gv, q, k, v = mixer_inputs(xn, w_in[l], gm_v_norm_g[l], q_norm_g[l], k_norm_g[l])
        gm = gmlp_chunk(gu, gv, gm_w_s[l], gm_b_s[l]).reshape(db, n, GM_WIDTH)
        k_all = jnp.concatenate([cache_sb_k[l], k], axis=1)
        v_all = jnp.concatenate([cache_sb_v[l], v], axis=1)
        past = cache_sb_k.shape[2]
        k_pos = jnp.arange(past + n, dtype=jnp.int32)
        q_pos = past + jnp.arange(n, dtype=jnp.int32)
        sb = stick_breaking(q, k_all, v_all, q_pos, k_pos).reshape(db, n, SB_WIDTH)
        h = ys + jnp.concatenate([gm, sb], axis=-1) @ w_out[l]
        ys = h + hier_moe(rmsnorm(h, norm2_g[l]), *moe_args)
        ks_list.append(k)
        vs_list.append(v)
        gv_list.append(gv)
    sb_k_prompt = jnp.stack(kp_list, axis=0)
    sb_v_prompt = jnp.stack(vp_list, axis=0)
    sb_k_sample = jnp.stack(ks_list, axis=0)
    sb_v_sample = jnp.stack(vs_list, axis=0)
    gm_v_sample = jnp.stack(gv_list, axis=0)
    return (yp, ys, sb_k_prompt, sb_v_prompt, sb_k_sample, sb_v_sample, gm_v_sample)


_drawn_inputs = setup_inputs


def setup_inputs(seed=0):
    import zlib

    import numpy as np

    out = dict(_drawn_inputs(seed))
    spreads = {}
    factors = {'gm_v_norm_g': 2.771,
     'gm_b_s': 3.438,
     'q_norm_g': 17.598,
     'b_router_group': 4.611,
     'b_router_expert': 4.771,
     'norm2_g': 3.153}
    for name, (base, spread) in spreads.items():
        noise = np.random.default_rng([zlib.crc32(name.encode()), seed]).standard_normal(out[name].shape)
        drawn = base * np.exp(spread * noise) if base else spread * noise
        out[name] = __import__('jax').numpy.asarray(drawn.astype(out[name].dtype))
    for name, factor in factors.items():
        out[name] = (out[name] * factor).astype(out[name].dtype)
    return out
```

```python
from contextlib import ExitStack

import concourse.bass as bass
from concourse import mybir
from concourse.alu_op_type import AluOpType as ALU

ACT = mybir.ActivationFunctionType
AX = mybir.AxisListType
F32 = mybir.dt.float32
F32R = mybir.dt.float32r
BF16 = mybir.dt.bfloat16
I32 = mybir.dt.int32
P = 128
EPS = 1e-6
NEG = -1e30


def trunk_step(nc, x_prompt, x_sample, cache_k, cache_v, norm1_g, w_in, gm_v_norm_g, gm_w_s, gm_b_s,
               q_norm_g, k_norm_g, w_out, norm2_g, w_rg, b_rg, w_re, b_re, w_gate, w_up, w_down,
               y_prompt, y_sample, k_prompt, v_prompt, k_sample, v_sample, gv_sample):
    SEQ, D = x_prompt.shape[1], x_prompt.shape[2]
    DEC = x_sample.shape[1]
    HEADS, HD = cache_k.shape[3], cache_k.shape[4]
    GROUPS = gm_w_s.shape[1]
    NG, EPG = w_re.shape[1], w_re.shape[3]
    E, FF = w_gate.shape[1], w_gate.shape[3]
    KC = D // P
    NT = SEQ // P + 1
    TOK = SEQ + DEC
    rows = [P] * (NT - 1) + [DEC]
    CB = 512
    UK = 4
    UNIT = UK * CB
    BLOCKS = ("gv", "u", "q", "k", "v")
    block_col = {"u": 0, "gv": CB, "q": 2 * CB, "k": 3 * CB, "v": 4 * CB}
    NB = len(BLOCKS)
    U_IN = 2 * NB
    U_ALL = U_IN + 2 * (D // CB)
    NCH = SEQ // P
    KCH = CB // P
    NE = NG + E
    CAP = 96
    ROUNDS = -(-TOK // CAP)
    SLOTS = E * CAP
    NRAW = 12
    BODY = 4
    AHEAD = 3
    assert FF * 2 == CB and D == 2 * CB and HEADS * HD == CB and SEQ == CB and E == 16

    xn_dram = nc.dram_tensor("normed_tokens", [TOK, D], F32, kind="Internal").ap()
    y_dram = nc.dram_tensor("expert_rows", [ROUNDS * SLOTS, D], F32, kind="Internal").ap()

    with ExitStack() as ctx:
        def sb(name, shape, dt=F32, stack=ctx):
            return stack.enter_context(nc.sbuf_tensor(name, shape, dt))

        def sem(name):
            return ctx.enter_context(nc.semaphore(name))

        bank = [ctx.enter_context(nc.psum_tensor(f"bank{i}", [P, 512], F32)) for i in range(8)]

        raw = [sb(f"raw{i}", [P, UNIT]) for i in range(3)]
        whi = [sb(f"whi{i}", [P, UNIT], F32R) for i in range(2)]
        wlo = [sb(f"wlo{i}", [P, UNIT], F32R) for i in range(2)]
        x_sb = sb("x_sb", [P, NT, D])
        ident = sb("ident", [P, P])
        identb = sb("identb", [P, P], BF16)
        maskneg = sb("maskneg", [P, P], BF16)
        maskneg8 = sb("maskneg8", [DEC, HEADS, DEC], BF16)
        negU = sb("negU", [P, P])
        negones = sb("negones", [P, P])
        before = sb("before", [P, P], BF16)
        onesb = sb("onesb", [P, P], BF16)
        ssq = sb("ssq", [P, 3, NT])
        rstd = sb("rstd", [P, 3, NT])
        ssq8 = sb("ssq8", [P, 2 * NT, HEADS])
        rstd8 = sb("rstd8", [P, 2 * NT, HEADS])
        mhalf = sb("mhalf", [P, HEADS])
        bs_col = sb("bs_col", [P, GROUPS])
        qg = sb("qg", [P, HD])
        kg = sb("kg", [P, HD])
        wr = sb("wr", [P, KC, NE])
        br = sb("br", [P, NE])
        tok_part = sb("tok_part", [P, 2, NT])
        valid = sb("valid", [P, NT])
        iota_i = sb("iota_i", [P, CAP], I32)
        slot_no = sb("slot_no", [P, CAP], BF16)
        iota_e = sb("iota_e", [P, E])
        prio = sb("prio", [P, EPG])
        lg = sb("lg", [P, NT, NE])
        r1 = [sb(f"r1_{i}", [P, NT]) for i in range(12)]
        selb = sb("selb", [P, NT, E], BF16)
        gate = [sb(f"gate{i}", [P, NT]) for i in range(2)]
        rank_of = [sb(f"rank_of{i}", [P, NT]) for i in range(2)]
        pos_y = [sb(f"pos_y{i}", [P, NT], I32) for i in range(2)]
        cnt = sb("cnt", [P, 1])
        flag = sb("flag", [P, 1], I32)
        idx_all = sb("idx_all", [CAP, E], I32)
        idx_cur = [sb(f"idx_cur{i}", [CAP, 1], I32) for i in range(2)]

        mix = ExitStack()
        xT_hi = sb("xT_hi", [P, KC, TOK], F32R, stack=mix)
        xT_lo = sb("xT_lo", [P, KC, TOK], F32R, stack=mix)
        qpad = sb("qpad", [P, HEADS, SEQ], stack=mix)
        qs = sb("qs", [P, KCH * P], stack=mix)
        kT = sb("kT", [P, KCH, TOK], stack=mix)
        v_sb = sb("v_sb", [P, NT, CB], stack=mix)
        gvn = sb("gvn", [P, NT, CB], stack=mix)
        ckT = sb("ckT", [P, KCH, SEQ], stack=mix)
        cv = sb("cv", [P, NCH, CB], stack=mix)
        ws = ckT[:, :, 0:P]
        st_a = ExitStack()
        xn = [sb(f"xn{i}", [P, D], stack=st_a) for i in range(2)]
        g1b = sb("g1b", [P, D], stack=st_a)
        sqt = [sb(f"sqt{i}", [P, CB], stack=st_a) for i in range(2)]
        gvb = sb("gvb", [P, CB], stack=st_a)
        WmT = sb("WmT", [P, GROUPS, P], stack=st_a)
        qn = [sb(f"qn{i}", [P, CB], stack=st_a) for i in range(2)]
        ut = qn
        st_a.close()
        st_b = ExitStack()
        ZW = 1280
        lw = [sb(f"lw{i}", [P, ZW], stack=st_b) for i in range(3)]
        sp = [sb(f"sp{i}", [P, ZW], stack=st_b) for i in range(2)]
        later = sb("later", [P, 6 * P], stack=st_b)
        st_b.close()
        st_c = ExitStack()
        sb("gap_c", [P, 512], stack=st_c)
        xn2 = [sb(f"xn2_{i}", [P, D], stack=st_c) for i in range(2)]
        g2b = sb("g2b", [P, D], stack=st_c)
        x2T = sb("x2T", [P, KC, P], stack=st_c)
        wr_pad = sb("wr_pad", [P, KC, P], stack=st_c)
        rk16 = [sb(f"rk16_{i}", [P, NT, E], stack=st_c) for i in range(2)]
        r4 = [sb(f"r4_{i}", [P, NT, EPG], stack=st_c) for i in range(6)]
        r16 = sb("r16", [P, NT, NG, EPG], stack=st_c)
        sel = [sb(f"sel{i}", [P, NT, NG, EPG], stack=st_c) for i in range(2)]
        st_c.close()
        mix.close()
        yout = [sb(f"yout{i}", [CAP, D]) for i in range(2)]
        late = [sb(f"raw{i}", [P, UNIT]) for i in range(9, NRAW)]
        onehot = sb("onehot", [P, 2 * NT, CAP], BF16)
        sb("gap_d", [P, 2 * KC * TOK - 4 * UNIT - NT * CAP])
        raw += [sb(f"raw{i}", [P, UNIT]) for i in range(3, 9)] + late
        whi.append(sb("whi2", [P, UNIT], F32R))
        wlo.append(sb("wlo2", [P, UNIT], F32R))
        xs = [sb(f"xs{i}", [CAP, D]) for i in range(2)]
        xsT_hi = [sb(f"xsT_hi{i}", [P, KC, CAP], F32R) for i in range(2)]
        xsT_lo = [sb(f"xsT_lo{i}", [P, KC, CAP], F32R) for i in range(2)]
        sg = [sb(f"sg{i}", [CAP, FF]) for i in range(2)]
        aT_hi = [sb(f"aT_hi{i}", [P, 2, CAP], F32R) for i in range(2)]
        aT_lo = [sb(f"aT_lo{i}", [P, 2, CAP], F32R) for i in range(2)]
        ids_of = sb("ids_of", [P, 2 * NT, 2 * E], BF16)
        idx_rows = sb("idx_rows", [CAP, E])
        yg = [[raw[2 * c + i][:, 0:D] for i in range(2)] for c in range(2)]

        ld_x = [sem(f"ld_x{t}") for t in range(NT)]
        ld_raw = [sem(f"ld_raw{i}") for i in range(3)]
        ld_g1, ld_ws, ld_gvb, ld_bs = sem("ld_g1"), sem("ld_ws"), sem("ld_gvb"), sem("ld_bs")
        ld_qg, ld_kg, ld_wr, ld_br = sem("ld_qg"), sem("ld_kg"), sem("ld_wr"), sem("ld_br")
        ld_ck = [sem(f"ld_ck{i}") for i in range(2)]
        ld_cv, ld_g2 = sem("ld_cv"), sem("ld_g2")
        pc = sem("pool_const")
        ws_masked = sem("ws_masked")
        ws_tr, wmT_ok = sem("ws_tr"), sem("wmT_ok")
        wr_padded = sem("wr_padded")
        ssq1_ok, rstd1_ok, xn_ok = sem("ssq1_ok"), sem("rstd1_ok"), sem("xn_ok")
        x_tr, xT_hi_ok, xT_lo_ok = sem("x_tr"), sem("xT_hi_ok"), sem("xT_lo_ok")
        ck_tr, ckT_ok = sem("ck_tr"), sem("ckT_ok")
        hi_ok, lo_ok = sem("hi_ok"), sem("lo_ok")
        half_done, proj_done = sem("half_done"), sem("proj_done")
        acc_free = [sem(f"acc_free{t}") for t in range(NT)]
        gv_gelu, gv_ssq, gv_rstd, gvn_ok = sem("gv_gelu"), sem("gv_ssq"), sem("gv_rstd"), sem("gvn_ok")
        u_gelu, mixed, gm_ok = sem("u_gelu"), sem("mixed"), sem("gm_ok")
        sq_ok, ssq8_ok, rstd8_ok = sem("sq_ok"), sem("ssq8_ok"), sem("rstd8_ok")
        qk_scaled, qk_ok, qk_tr, qkT_ok = sem("qk_scaled"), sem("qk_ok"), sem("qk_tr"), sem("qkT_ok")
        v_ok = sem("v_ok")
        k_out = [sem(f"k_out{i}") for i in range(2)]
        st_out = sem("st_out")
        gm_tr, gmT_hi, gmT_lo = sem("gm_tr"), sem("gmT_hi"), sem("gmT_lo")
        z_ok, az_ok, e_ok, l_ok, sp_ok = sem("z_ok"), sem("az_ok"), sem("e_ok"), sem("l_ok"), sem("sp_ok")
        later_ok = sem("later_ok")
        rest_ok, w_ok, pv_ok, sbT_hi, sbT_lo = sem("rest_ok"), sem("w_ok"), sem("pv_ok"), sem("sbT_hi"), sem("sbT_lo")
        h_ok, ssq2_ok, rstd2_ok, xn2_ok = sem("h_ok"), sem("ssq2_ok"), sem("rstd2_ok"), sem("xn2_ok")
        xn_st = [sem(f"xn_st{i}") for i in range(2)]
        x2_tr, x2T_ok, r_mm, lg_ok = sem("x2_tr"), sem("x2T_ok"), sem("r_mm"), sem("lg_ok")
        rx, r_exp = sem("router_to_act"), sem("router_exp")
        selb_ok, rank_ok, flag_ok = sem("selb_ok"), sem("rank_ok"), sem("flag_ok")
        rank_less, onehot_ok, ids_mm = sem("rank_less"), sem("onehot_ok"), sem("ids_mm")
        idx_half, idx_ok, idx_cp, places_ok = sem("idx_half"), sem("idx_ok"), sem("idx_cp"), sem("places_ok")
        m_ld = [sem(f"m_ld{i}") for i in range(NRAW)]
        m_hi, m_lo, m_lo_pool, m_used = sem("m_hi"), sem("m_lo"), sem("m_lo_pool"), sem("m_used")
        xs_ld = [sem(f"xs_ld{i}") for i in range(2)]
        xs_tr, xsT_hi_ok, xsT_lo_ok = sem("xs_tr"), sem("xsT_hi_ok"), sem("xsT_lo_ok")
        silu_ok, a_ok, a_tr, aT_hi_ok, aT_lo_ok = (sem(n) for n in ("silu_ok", "a_ok", "a_tr", "aT_hi_ok", "aT_lo_ok"))
        y_act, y_dve = sem("y_act"), sem("y_dve")
        y_st = [sem(f"y_st{i}") for i in range(2)]
        yg_ld = [sem(f"yg_ld{i}") for i in range(2)]
        y_ok, y_out = sem("y_ok"), sem("y_out")
        dch, pch = sem("dve_chain"), sem("pool_chain")
        pool_tick, sp_tick = sem("pool_tick"), sem("sp_tick")

        def tok(t):
            return slice(t * P, t * P + rows[t])

        X_USE, CK_USE = 0, 2 * NT
        QK_USE = CK_USE + NCH
        GM_USE = QK_USE + 2 * NT
        PV_USE = GM_USE + NT

        def turn_bank(use):
            return bank[5 + use % 2]

        def wait_turn(pe, use):
            u = use - 2
            if u < 0:
                return
            if u < CK_USE:
                pe.wait_ge(xT_lo_ok, u + 1)
            elif u < QK_USE:
                pe.wait_ge(ckT_ok, u - CK_USE + 1)
            elif u < GM_USE:
                pe.wait_ge(qkT_ok, u - QK_USE + 1)
            elif u < PV_USE:
                pe.wait_ge(gmT_lo, u - GM_USE + 1)
            else:
                pe.wait_ge(sbT_lo, u - PV_USE + 1)

        z_sets = [[bank[0], bank[1], bank[2]], [bank[3], bank[4], bank[7]]]
        regions = [(0, 0, 512, 0, 0), (1, 0, 384, 1, 128), (1, 384, 128, 3, 384), (2, 0, 256, 2, 256)]
        DW = HEADS * DEC
        s_regions = [(c * DW // 512, c * DW % 512, DW, c) for c in range(NCH + 1)]
        NH = HEADS + 1

        def later_sums(h):
            return later[:, 3 * P * (h % 2):3 * P * (h % 2 + 1)] if h < HEADS else later[:, :]

        def pairs(a, odd, side):
            c = odd * (P + 2 * DEC) + side * DEC
            return a.rearrange("p (w c) -> p w c", c=2 * P)[:, :, c:c + DEC]

        SPLIT_OF = (0, 2, 1)

        def unit_at(i, c, j, a):
            m = 3 * i - 1 + c if isinstance(i, int) else 3 * (3 + a) - 1 + c
            return m % NRAW, (0 if isinstance(i, int) else j) + m // NRAW

        def half_of(i, j, a):
            return i // 2 if isinstance(i, int) else 2 * j + a // 2

        def gate_up_used(i):
            return 2 if isinstance(i, int) and i == 0 else 3 * i + 1

        def down_used(i):
            return 3 * E if isinstance(i, int) and i == E - 1 else 3 * i + 5

        K_STORED = [16 * sum(m % 2 == i for m in range(NT, 2 * NT)) for i in range(2)]
        PC_IDENT, PC_MASK, PC_U, PC_B, PC_QPAD, PC_R = 1, 2, 3, 4, 5, 6

        def unit_used(eng, n):
            if n % 2 == 0:
                eng.wait_ge(half_done, n // 2 + 1)
            else:
                eng.wait_ge(proj_done, NT * (n // 2 + 1))

        block = ctx.enter_context(nc.Block())

        @block.sync
        def _(sp_):
            for t in range(NT):
                src = x_prompt[0, tok(t), :] if t < NT - 1 else x_sample[0, :, :]
                sp_.dma_start(x_sb[0:rows[t], t, :], src).then_inc(ld_x[t], 16)

            def load_unit(n):
                if n >= 3:
                    sp_.wait_ge(hi_ok, n - 2)
                    sp_.wait_ge(lo_ok, n - 2)
                if n < U_IN:
                    src, c0, half = w_in, block_col[BLOCKS[n // 2]], n % 2
                else:
                    src, c0, half = w_out, CB * ((n - U_IN) // 2), n % 2
                view = src[0, half * UK * P:(half + 1) * UK * P, c0:c0 + CB].rearrange("(k p) n -> p k n", p=P)
                sp_.dma_start(raw[n % 3][:, :].rearrange("p (k n) -> p k n", k=UK), view).then_inc(ld_raw[n % 3], 16)

            for n in range(U_ALL):
                load_unit(n)

            def load_gate_up(e, half, slot):
                dst = raw[slot][:, :].rearrange("p (k n) -> p k n", k=UK)
                for j, w in enumerate((w_gate, w_up)):
                    src = w[0, e, half * UK * P:(half + 1) * UK * P, :].rearrange("(k p) f -> p k f", p=P)
                    sp_.dma_start(dst[:, :, j * FF:(j + 1) * FF], src).then_inc(m_ld[slot], 16)

            def load_down(e, slot):
                for k in range(2):
                    sp_.dma_start(raw[slot][:, k * D:(k + 1) * D], w_down[0, e, k * P:(k + 1) * P, :])\
                       .then_inc(m_ld[slot], 16)

            def moe_loads(r):
                u0 = 3 * E * r

                def raw_free(m):
                    if isinstance(r, int) and isinstance(m, int) and m < NRAW:
                        if m < 3:
                            sp_.wait_ge(hi_ok, (U_ALL - 1, U_ALL, U_ALL - 2)[m])
                            sp_.wait_ge(lo_ok, (U_ALL - 1, U_ALL, U_ALL - 2)[m])
                        elif m < 9:
                            sp_.wait_ge(pv_ok, NH)
                            sp_.wait_ge(gmT_lo, NT)
                            sp_.wait_ge(st_out, 16 * (NT + 1))
                        else:
                            sp_.wait_ge(proj_done, NT * (NB + 2))
                    else:
                        n = u0 + m - (NRAW - 1)
                        sp_.wait_ge(m_hi, n)
                        sp_.wait_ge(m_lo, n)
                        sp_.sem_inc(sp_tick, 1)

                def gate_up_unit(i, half, m, slot):
                    raw_free(m)
                    load_gate_up(i, half, slot)

                def down_unit(i, m, slot):
                    raw_free(m)
                    load_down(i, slot)

                def first(m):
                    i = (m + 1) // 3
                    if not isinstance(r, int):
                        if m % 3 == 1:
                            sp_.wait_ge(m_lo_pool, (E + 1) * r - 4 + m // 3)
                            sp_.sem_inc(sp_tick, 1)
                        elif m == NRAW - 1:
                            sp_.wait_ge(m_lo_pool, (E + 1) * r)
                            sp_.sem_inc(sp_tick, 1)
                    if m < 2:
                        gate_up_unit(0, m, m, m)
                    elif (m + 1) % 3 == 2:
                        down_unit(i - 1, m, m)
                    else:
                        gate_up_unit(i, (m + 1) % 3, m, m)

                def few_in_flight(i, b, c):
                    u = 3 * b + c - AHEAD
                    group = i // BODY if isinstance(i, int) else (i - b) // BODY
                    sp_.wait_ge(m_ld[u % NRAW], 32 * (3 * E // NRAW * r + group + 1 + u // NRAW))
                    sp_.sem_inc(sp_tick, 1)

                def step(i, b):
                    m = 3 * i
                    few_in_flight(i, b, 0)
                    gate_up_unit(i, 1, m, 3 * b)
                    few_in_flight(i, b, 1)
                    sp_.wait_ge(m_lo_pool, (E + 1) * r + i - 3)
                    sp_.sem_inc(sp_tick, 1)
                    down_unit(i - 1, m + 1, 3 * b + 1)
                    few_in_flight(i, b, 2)
                    gate_up_unit(i + 1, 0, m + 2, 3 * b + 2)

                for m in (2, 0, 3, 4, 5, 6, 1, 7, 8, 9, 10, 11):
                    first(m)
                with sp_.Fori(1, E // BODY - 1) as j:
                    for b in range(BODY):
                        step(BODY * j + b, b)
                for b in range(BODY - 1):
                    step(E - BODY + b, b)
                gate_up_unit(E - 1, 1, 3 * E - 3, NRAW - 3)
                sp_.wait_ge(m_lo_pool, (E + 1) * r + E - 4)
                sp_.sem_inc(sp_tick, 1)
                down_unit(E - 2, 3 * E - 2, NRAW - 2)
                down_unit(E - 1, 3 * E - 1, NRAW - 1)

            moe_loads(0)
            sp_.wait_ge(flag_ok, 1)
            more = sp_.value_load(flag[0:1, 0:1], min_val=0, max_val=1)
            with sp_.If(more != 0):
                with sp_.Fori(1, ROUNDS) as r:
                    moe_loads(r)
            for t in range(NT):
                sp_.wait_ge(y_ok, t + 1)
                dst = y_prompt[0, tok(t), :] if t < NT - 1 else y_sample[0, :, :]
                sp_.dma_start(dst, x_sb[0:rows[t], t, :]).then_inc(y_out, 16)
            sp_.wait_ge(y_out, 16 * NT)

        @block.gpsimd
        def _(pool):
            chain = [0]

            def link(ins):
                chain[0] += 1
                ins.then_inc(pch, 1)
                pool.wait_ge(pch, chain[0])

            pool.dma_start(ws, gm_w_s[0].rearrange("g t s -> t g s")).then_inc(ld_ws, 16)
            link(pool.memset(ident[:, :], 0.0))
            link(pool.affine_select(out=ident[:, :], in_=ident[:, :], compare_op=ALU.not_equal, fill=1.0, base=0,
                                    pattern=[[-1, P]], channel_multiplier=1))
            pool.tensor_copy(identb[:, :], ident[:, :]).then_inc(pc, 1)
            pool.wait_ge(ld_ws, 16)
            pool.affine_select(out=ws, in_=ws, compare_op=ALU.is_ge, fill=0.0, base=0,
                               pattern=[[0, GROUPS], [-1, P]], channel_multiplier=1).then_inc(ws_masked, 1)
            link(pool.memset(mhalf[:, :], -0.5))

            def inv_root(dst, s, width):
                link(pool.tensor_scalar(s, s, 1.0 / width, EPS, ALU.mult, ALU.add))
                n = s.shape[-1]
                return pool.tensor_tensor(dst, s, mhalf[0:s.shape[0], 0:n], ALU.pow)

            for t in range(NT):
                pool.wait_ge(ssq1_ok, t + 1)
                inv_root(rstd[0:rows[t], 0, t:t + 1], ssq[0:rows[t], 0, t:t + 1], D).then_inc(rstd1_ok, 1)

            link(pool.memset(maskneg[:, :], 0.0))
            link(pool.affine_select(out=maskneg[:, :], in_=maskneg[:, :], compare_op=ALU.is_gt, fill=NEG, base=0,
                                    pattern=[[1, P]], channel_multiplier=-1))
            for h in range(HEADS):
                ins = pool.tensor_copy(maskneg8[:, h, :], maskneg[0:DEC, 0:DEC])
            ins.then_inc(pc, 1)
            link(pool.memset(negU[:, :], -1.0))
            pool.memset(negones[:, :], -1.0)
            pool.affine_select(out=negU[:, :], in_=negU[:, :], compare_op=ALU.is_ge, fill=0.0, base=0,
                               pattern=[[-1, P]], channel_multiplier=1).then_inc(pc, 1)
            link(pool.memset(before[:, :], 1.0))
            pool.memset(onesb[:, :], 1.0)
            pool.affine_select(out=before[:, :], in_=before[:, :], compare_op=ALU.is_gt, fill=0.0, base=0,
                               pattern=[[1, P]], channel_multiplier=-1).then_inc(pc, 1)
            pool.memset(qs[:, :], 0.0)
            pool.memset(qpad[:, :, :], 0.0).then_inc(pc, 1)
            link(pool.iota(iota_i[:, :], pattern=[[1, CAP]], base=0, channel_multiplier=0))
            link(pool.tensor_copy(iota_e[:, :], iota_i[:, 0:E]))
            pool.tensor_scalar(prio[:, :], iota_e[:, 0:EPG], -1.0, float(EPG), ALU.mult, ALU.add)
            link(pool.tensor_copy(slot_no[:, :], iota_i[:, :]))
            pool.iota(iota_i[:, 0:NT], pattern=[[0, NT]], base=0, channel_multiplier=1)
            link(pool.iota(iota_i[:, NT:2 * NT], pattern=[[P, NT]], base=0, channel_multiplier=0))
            link(pool.tensor_copy(tok_part[:, :, :], iota_i[:, 0:2 * NT].rearrange("p (a t) -> p a t", a=2)))
            for a in range(2):
                pool.affine_select(out=tok_part[:, a, :], in_=tok_part[:, a, :], compare_op=ALU.is_ge, fill=0.0, base=TOK - 1,
                                   pattern=[[-P, NT]], channel_multiplier=-1)
            link(pool.memset(valid[:, :], 1.0))
            pool.affine_select(out=valid[:, :], in_=valid[:, :], compare_op=ALU.is_ge, fill=0.0, base=TOK - 1,
                               pattern=[[-P, NT]], channel_multiplier=-1).then_inc(pc, 1)

            for t in range(NT):
                pool.wait_ge(gv_ssq, t + 1)
                inv_root(rstd[0:rows[t], 1, t:t + 1], ssq[0:rows[t], 1, t:t + 1], CB).then_inc(gv_rstd, 1)
            pool.wait_ge(gvn_ok, NT)
            pool.dma_start(gv_sample[0, 0].rearrange("t g d -> t (g d)"), gvn[0:DEC, NT - 1, :]).then_inc(st_out, 16)

            for b in range(2):
                pool.wait_ge(ld_kg if b else ld_qg, 16)
                if b == 0:
                    link(pool.tensor_scalar(qg[:, :], qg[:, :], HD ** -0.5, 0.0, ALU.mult, ALU.add))
                for t in range(NT):
                    m, p = NT * b + t, rows[t]
                    pool.wait_ge(ssq8_ok, m + 1)
                    inv_root(rstd8[0:p, m, :], ssq8[0:p, m, :], HD).then_inc(rstd8_ok, 1)
                    pool.wait_ge(qk_scaled, m + 1)
                    q3 = qn[m % 2][0:p, :].rearrange("p (h d) -> p h d", h=HEADS)
                    g = (kg if b else qg)[0:p, :].rearrange("p (a d) -> p a d", a=1).broadcast_to([p, HEADS, HD])
                    pool.tensor_tensor(q3, q3, g, ALU.mult).then_inc(qk_ok, 1)
                    if b:
                        dst = k_prompt[0, 0, tok(t)] if t < NT - 1 else k_sample[0, 0]
                        pool.wait_ge(qk_ok, m + 1)
                        pool.dma_start(dst.rearrange("t h d -> t (h d)"), qn[m % 2][0:p, :]).then_inc(k_out[m % 2], 16)
            for t in range(NT):
                dst = v_prompt[0, 0, tok(t)] if t < NT - 1 else v_sample[0, 0]
                pool.wait_ge(v_ok, t + 1)
                pool.dma_start(dst.rearrange("t h d -> t (h d)"), v_sb[0:rows[t], t, :]).then_inc(st_out, 16)

            pool.wait_ge(w_ok, NH)
            pool.wait_ge(pv_ok, NH)
            pool.wait_ge(ld_wr, 16 * (NG + 1))
            link(pool.memset(wr_pad[:, :, :], 0.0))
            pool.tensor_copy(wr_pad[:, :, 0:NE], wr[:, :, :]).then_inc(wr_padded, 1)
            pool.dma_start(g2b[:, :], norm2_g.broadcast_to([P, D])).then_inc(ld_g2, 16)
            for t in range(NT):
                pool.wait_ge(ssq2_ok, t + 1)
                inv_root(rstd[0:rows[t], 2, t:t + 1], ssq[0:rows[t], 2, t:t + 1], D).then_inc(rstd2_ok, 1)
                pool.wait_ge(xn2_ok, t + 1)
                pool.dma_start(xn_dram[tok(t), :], xn2[t % 2][0:rows[t], :]).then_inc(xn_st[t % 2], 16)

            for i in range(2):
                pool.wait_ge(xn_st[i], 16 * ((NT + 1 - i) // 2))

            def moe_gathers(r):
                s0, u0 = E * r, 3 * E * r
                for m in range(3):
                    pool.wait_ge(m_hi, u0 + m + 1)
                    pool.sem_inc(pool_tick, 1)
                    pool.tensor_tensor(wlo[SPLIT_OF[m]][:, :], raw[m][:, :], whi[SPLIT_OF[m]][:, :].bitcast(F32), ALU.subtract)\
                        .then_inc(m_lo, 1)
                pool.wait_ge(idx_ok, r + 1)
                pool.sem_inc(pool_tick, 1)

                def gather(i, p):
                    s = s0 + i
                    if not (isinstance(s, int) and s < 2):
                        pool.wait_ge(xs_tr, 2 * (s - 1))
                        pool.sem_inc(pool_tick, 1)
                    pool.tensor_copy(idx_cur[p][:, :], idx_all[:, bass.ds(i, 1)]).then_inc(idx_cp, 1)
                    pool.wait_ge(idx_cp, s + 1)
                    pool.sem_inc(pool_tick, 1)
                    pool.indirect_dma_start(xs[p][:, :], None, xn_dram[:, :],
                                            bass.IndirectOffsetOnAxis(ap=idx_cur[p][:, 0:1], axis=0)).then_inc(xs_ld[p], 16)

                def lo(i, j, a):
                    m = 3 * i + 1 if not (isinstance(i, int) and i == E) else 3 * E - 1
                    slot = unit_at(i, 2, j, a)[0] if not (isinstance(i, int) and i == E) else (3 * E - 1) % NRAW
                    split = SPLIT_OF[1] if not (isinstance(i, int) and i == E) else SPLIT_OF[2]
                    pool.wait_ge(m_hi, u0 + m + 1)
                    pool.sem_inc(pool_tick, 1)
                    pool.tensor_tensor(wlo[split][:, D:2 * D], raw[slot][:, D:2 * D], whi[split][:, D:2 * D].bitcast(F32),
                                       ALU.subtract).then_inc(m_lo_pool, 1)

                def store(i, p):
                    s = s0 + i
                    pool.wait_ge(y_act, s + 1)
                    pool.wait_ge(y_dve, s + 1)
                    pool.dma_start(y_dram[bass.ds(r * SLOTS + i * CAP, CAP), :], yout[p][:, :]).then_inc(y_st[p], 16)

                def step(i, j, a, p):
                    if isinstance(i, int) and i == 0:
                        pool.sem_inc(m_lo_pool, 1)
                    else:
                        lo(i, j, a)
                    if not (isinstance(i, int) and i >= E - 2):
                        gather(i + 2, p)
                    if not (isinstance(i, int) and i < 2):
                        store(i - 2, p)

                gather(0, 0)
                gather(1, 1)
                for i in range(3):
                    step(i, 0, 0, i % 2)
                with pool.Fori(0, (E - 4) // BODY - 1) as j:
                    for a in range(BODY):
                        step(BODY * j + 3 + a, j, a, (3 + a) % 2)
                for i in range(E - 1 - BODY, E):
                    step(i, 0, 0, i % 2)
                lo(E, 0, 0)
                store(E - 2, 0)
                store(E - 1, 1)
                for p in range(2):
                    pool.wait_ge(y_st[p], 16 * (E // 2) * (r + 1))

            def fetch(n):
                pool.wait_ge(places_ok, 1)
                for t in range(NT):
                    if t >= 2:
                        pool.wait_ge(y_ok, t - 1)
                    for c in range(2):
                        pool.indirect_dma_start(yg[c][t % 2][0:rows[t], :], None, y_dram[0:n, :],
                                                bass.IndirectOffsetOnAxis(ap=pos_y[c][0:rows[t], t:t + 1], axis=0))\
                            .then_inc(yg_ld[t % 2], 16)

            moe_gathers(0)
            pool.wait_ge(flag_ok, 1)
            more = pool.value_load(flag[0:1, 0:1], min_val=0, max_val=1)
            with pool.If(more != 0):
                with pool.Fori(1, ROUNDS) as r:
                    moe_gathers(r)
                fetch(ROUNDS * SLOTS)
            with pool.Else():
                fetch(SLOTS)
            pool.wait_ge(st_out, 16 * (NT + 1))
            for i in range(2):
                pool.wait_ge(k_out[i], K_STORED[i])

        @block.scalar
        def _(act):
            act.dma_start(g1b[:, :], norm1_g.broadcast_to([P, D])).then_inc(ld_g1, 16)
            act.dma_start(gvb[:, :], gm_v_norm_g.broadcast_to([P, CB])).then_inc(ld_gvb, 16)
            act.dma_start(qg[:, :], q_norm_g.broadcast_to([P, HD])).then_inc(ld_qg, 16)
            act.dma_start(kg[:, :], k_norm_g.broadcast_to([P, HD])).then_inc(ld_kg, 16)
            act.dma_start(bs_col[:, :], gm_b_s[0].rearrange("g t -> t g"), allow_slow_non_contiguous=True).then_inc(ld_bs, 16)
            act.dma_start(cv[:, :, :], cache_v[0, 0].rearrange("(c p) h d -> p c (h d)", p=P)).then_inc(ld_cv, 16)
            act.dma_start(wr[:, :, 0:NG], w_rg[0].rearrange("(k p) g -> p k g", p=P)).then_inc(ld_wr, 16)
            for g in range(NG):
                act.dma_start(wr[:, :, NG + g * EPG:NG + (g + 1) * EPG], w_re[0, g].rearrange("(k p) e -> p k e", p=P))\
                   .then_inc(ld_wr, 16)
            act.dma_start(br[:, 0:NG], b_rg.broadcast_to([P, NG])).then_inc(ld_br, 16)
            act.dma_start(br[:, NG:NE], b_re.rearrange("l g e -> l (g e)").broadcast_to([P, E])).then_inc(ld_br, 16)

            def split_hi(n):
                act.wait_ge(ld_raw[n % 3], 16 * (n // 3 + 1))
                if n >= 2:
                    unit_used(act, n - 2)
                act.activation(whi[n % 2][:, :], raw[n % 3][:, :], ACT.Copy).then_inc(hi_ok, 1)

            act.wait_ge(ws_tr, 1)
            act.activation(WmT[:, :, :].rearrange("p g s -> p (g s)"), bank[7][:, :], ACT.Copy).then_inc(wmT_ok, 1)
            for t in range(NT):
                for b in range(2):
                    act.wait_ge(x_tr, 2 * t + b + 1)
                    src = turn_bank(X_USE + 2 * t + b)[:, :].rearrange("p (k n) -> p k n", k=4)[:, :, 0:rows[t]]
                    act.activation(xT_hi[:, 4 * b:4 * b + 4, tok(t)], src, ACT.Copy).then_inc(xT_hi_ok, 1)
            for c2 in range(2):
                act.dma_start(xn[c2][:, :].rearrange("p (c n) -> p c n", c=2),
                              cache_k[0, 0, 2 * c2 * P:2 * (c2 + 1) * P].rearrange("(c p) h d -> p c (h d)", p=P))\
                   .then_inc(ld_ck[c2], 16)
            split_hi(0)
            split_hi(1)
            for b, name in enumerate(BLOCKS):
                if name in ("k", "v"):
                    for t in range(NT):
                        m = NT * (name == "v") + t
                        act.wait_ge(qk_tr, m + 1)
                        src = turn_bank(QK_USE + m)[:, :].rearrange("p (j n) -> p j n", j=KCH)[:, :, 0:rows[t]]
                        if name == "v":
                            act.activation(kT[:, :, tok(t)], src, ACT.Copy).then_inc(qkT_ok, 1)
                        else:
                            if t == 0:
                                act.wait_ge(pc, PC_QPAD)
                            if t < NT - 1:
                                q4 = qpad[:, :, :].rearrange("p (j a) n -> p j a n", a=2)
                                act.activation(q4[0:HD, :, 0, tok(t)], src[0:HD], ACT.Copy)
                                act.activation(q4[HD:P, :, 1, tok(t)], src[HD:P], ACT.Copy).then_inc(qkT_ok, 1)
                            else:
                                for odd in range(2):
                                    act.activation(pairs(qs[0:HD, :], odd, 0), src[0:HD, odd:KCH:2], ACT.Copy)
                                    ins = act.activation(pairs(qs[HD:P, :], odd, 1), src[HD:P, odd:KCH:2], ACT.Copy)
                                ins.then_inc(qkT_ok, 1)
                split_hi(2 * b + 2)
                for t in range(NT):
                    p = rows[t]
                    act.wait_ge(proj_done, NT * b + t + 1)
                    a = bank[t][0:p, :]
                    if name == "gv":
                        act.activation(gvn[0:p, t, :], a, ACT.Gelu_apprx_tanh).then_inc(gv_gelu, 1)
                    elif name == "u":
                        if t >= 2:
                            act.wait_ge(gm_ok, t - 1)
                        act.activation(ut[t % 2][0:p, :], a, ACT.Gelu_apprx_tanh).then_inc(acc_free[t], 1)
                    elif name in ("q", "k"):
                        m = NT * (b - 2) + t
                        if m >= 2:
                            act.wait_ge(ssq8_ok, m - 1)
                        act.activation(sqt[m % 2][0:p, :], a, ACT.Square).then_inc(sq_ok, 1)
                    else:
                        act.activation(v_sb[0:p, t, :], a, ACT.Copy).then_inc(v_ok, 1)
                if b == 0:
                    for c in range(NCH):
                        act.wait_ge(ck_tr, c + 1)
                        act.activation(ckT[:, :, c * P:(c + 1) * P],
                                       turn_bank(CK_USE + c)[:, :].rearrange("p (j n) -> p j n", j=KCH), ACT.Copy)\
                           .then_inc(ckT_ok, 1)
                split_hi(2 * b + 3)

            def exp_log(h):
                act.wait_ge(az_ok, h + 1)
                b_ = lw[h % 3]
                parts = [b_[:, :]] if h < HEADS else [b_[:, 0:1024], b_[0:DEC, 1024:ZW]]
                for n, a in enumerate(parts):
                    ins = act.activation(a, a, ACT.Exp, scale=-1.0)
                ins.then_inc(e_ok, 1)
                act.wait_ge(e_ok, h + 1)
                for a in parts:
                    ins = act.activation(a, a, ACT.Ln, bias=1.0)
                ins.then_inc(l_ok, 1)

            def weights(h):
                act.wait_ge(rest_ok, h + 1)
                z = z_sets[h % 2]
                act.wait_ge(sp_ok, h + 1)
                act.activation(lw[h % 3][:, 0:512], z[0][:, :], ACT.Exp)
                act.activation(lw[h % 3][:, 512:1024], z[1][:, :], ACT.Exp)
                p = P if h < HEADS else DEC
                act.activation(lw[h % 3][0:p, 1024:ZW], z[2][0:p, 0:256], ACT.Exp).then_inc(w_ok, 1)

            def sb_hi(h):
                act.wait_ge(pv_ok, h + 1)
                o = turn_bank(PV_USE + h)
                if h < HEADS:
                    r0 = HD * (h % 2)
                    act.activation(xT_hi[r0:r0 + HD, KCH + h // 2, 0:SEQ], o[0:HD, :], ACT.Copy).then_inc(sbT_hi, 1)
                else:
                    for odd in range(2):
                        for a in range(2):
                            r = slice(HD * a, HD * (a + 1))
                            ins = act.activation(xT_hi[r, KCH + odd:KC:2, SEQ:TOK], pairs(o[r, :], odd, a), ACT.Copy)
                    ins.then_inc(sbT_hi, 1)

            act.preload_act_table_set("natural_log_exp_and_others")
            exp_log(0)
            for t in range(NT):
                act.wait_ge(gm_tr, t + 1)
                src = turn_bank(GM_USE + t)[:, :].rearrange("p (k n) -> p k n", k=KCH)[:, :, 0:rows[t]]
                act.activation(xT_hi[:, 0:KCH, tok(t)], src, ACT.Copy).then_inc(gmT_hi, 1)
            for h in range(NH):
                if h + 1 < NH:
                    exp_log(h + 1)
                weights(h)
                if h >= 1:
                    sb_hi(h - 1)
            sb_hi(NH - 1)

            split_hi(U_IN + 2)
            split_hi(U_IN + 3)
            def first_hi(m):
                act.wait_ge(m_ld[m], 32)
                act.activation(whi[SPLIT_OF[m]][:, :], raw[m][:, :], ACT.Copy).then_inc(m_hi, 1)

            unit_used(act, U_IN + 2)
            first_hi(0)
            first_hi(1)
            for t in range(NT):
                if t == NT - 1:
                    unit_used(act, U_IN + 3)
                    first_hi(2)
                for b in range(2):
                    act.wait_ge(x2_tr, 2 * t + b + 1)
                    if t >= 1 and b == 0:
                        act.wait_ge(r_mm, t)
                    src = bank[5 + b][:, :].rearrange("p (k n) -> p k n", k=4)[:, :, 0:rows[t]]
                    act.activation(x2T[:, 4 * b:4 * b + 4, 0:rows[t]], src, ACT.Copy).then_inc(x2T_ok, 1)
            act.wait_ge(rx, 1)
            act.activation(r4[1][:, :, :], r4[0][:, :, :], ACT.Exp).then_inc(r_exp, 1)
            act.wait_ge(rx, 2)
            act.activation(r1[5][:, :], r1[4][:, :], ACT.Exp).then_inc(r_exp, 1)
            act.preload_act_table_set("silu_and_others")

            def moe(r):
                s0, u0 = E * r, 3 * E * r

                def hi(m3, at, unit):
                    slot, group = at
                    act.wait_ge(m_ld[slot], 32 * (3 * E // NRAW * r + group + 1))
                    if not (isinstance(unit, int) and unit < 3):
                        act.wait_ge(m_used, unit - 2)
                    act.activation(whi[SPLIT_OF[m3]][:, :], raw[slot][:, :], ACT.Copy).then_inc(m_hi, 1)

                def tokens_hi(i, p):
                    s = s0 + i
                    for b in range(2):
                        act.wait_ge(xs_tr, 2 * s + b + 1)
                        if b == 0 and not (isinstance(i, int) and i < 2):
                            act.wait_ge(m_used, u0 + gate_up_used(i - 2))
                        act.activation(xsT_hi[p][:, 4 * b:4 * b + 4, :].rearrange("p k n -> p (k n)"),
                                       bank[5 + b][:, 0:4 * CAP], ACT.Copy).then_inc(xsT_hi_ok, 1)

                def silu(i, p):
                    s = s0 + i
                    act.wait_ge(m_used, u0 + gate_up_used(i))
                    if not (isinstance(s, int) and s < 2):
                        act.wait_ge(a_tr, s - 1)
                    act.activation(sg[p][:, :], bank[p][0:CAP, 0:FF], ACT.Silu).then_inc(silu_ok, 1)

                def act_hi(i, p):
                    s = s0 + i
                    act.wait_ge(a_tr, s + 1)
                    if not (isinstance(i, int) and i < 2):
                        act.wait_ge(m_used, u0 + down_used(i - 2))
                    act.activation(aT_hi[p][:, :, :].rearrange("p k n -> p (k n)"), bank[7][:, 0:2 * CAP], ACT.Copy)\
                       .then_inc(aT_hi_ok, 1)

                def out_rows(i, p, n):
                    act.wait_ge(m_used, u0 + down_used(i))
                    if not (isinstance(r, int) and isinstance(i, int) and i < 2):
                        act.wait_ge(y_st[p], 16 * ((E // 2) * r + n))
                    act.activation(yout[p][:, 0:CB], bank[2][0:CAP, :], ACT.Copy).then_inc(y_act, 1)

                def step(i, j, a):
                    first = isinstance(i, int) and i == 0
                    last = isinstance(i, int) and i == E - 1
                    p = i % 2 if isinstance(i, int) else (3 + a) % 2
                    if not first:
                        hi(1, unit_at(i, 2, j, a), u0 + 3 * i + 1)
                        act_hi(i - 1, 1 - p)
                    if not first:
                        hi(2, unit_at(i, 3, j, a), u0 + 3 * i + 2)
                    if not last:
                        tokens_hi(i + 1, 1 - p)
                    silu(i, p)
                    if not last:
                        hi(0, unit_at(i, 4, j, a), u0 + 3 * i + 3)
                    if not first:
                        out_rows(i - 1, 1 - p, half_of(i - 1, j, 2 + a))

                if not isinstance(r, int):
                    for m in range(3):
                        hi(m, (m, 0), u0 + m)
                tokens_hi(0, 0)
                for i in range(3):
                    step(i, 0, 0)
                with act.Fori(0, (E - 4) // BODY) as j:
                    for a in range(BODY):
                        step(BODY * j + 3 + a, j, a)
                step(E - 1, 0, 0)
                act_hi(E - 1, 1)
                out_rows(E - 1, 1, E // 2 - 1)

            moe(0)
            act.wait_ge(flag_ok, 1)
            more = act.value_load(flag[0:1, 0:1], min_val=0, max_val=1)
            with act.If(more != 0):
                with act.Fori(1, ROUNDS) as r:
                    moe(r)

        @block.vector
        def _(dve):
            chain = [0]

            def link(ins):
                chain[0] += 1
                ins.then_inc(dch, 1)
                dve.wait_ge(dch, chain[0])

            def split_lo(n):
                dve.wait_ge(hi_ok, n + 1)
                dve.tensor_tensor(wlo[n % 2][:, :], raw[n % 3][:, :], whi[n % 2][:, :].bitcast(F32), ALU.subtract)\
                   .then_inc(lo_ok, 1)

            def square_sum(dst, x, junk):
                return dve.tensor_tensor_reduce(junk, x, x, 1.0, 0.0, ALU.mult, ALU.add, dst)

            def norm_x(t):
                p = rows[t]
                dve.wait_ge(rstd1_ok, t + 1)
                if t == 0:
                    dve.wait_ge(ld_g1, 16)
                dve.scalar_tensor_tensor(out=xn[t % 2][0:p, :], in0=x_sb[0:p, t, :], scalar=rstd[0:p, 0, t:t + 1],
                                         in1=g1b[0:p, :], op0=ALU.mult, op1=ALU.mult).then_inc(xn_ok, 1)

            def x_lo(t):
                for b in range(2):
                    dve.wait_ge(xT_hi_ok, 2 * t + b + 1)
                    src = turn_bank(X_USE + 2 * t + b)[:, :].rearrange("p (k n) -> p k n", k=4)[:, :, 0:rows[t]]
                    dve.tensor_tensor(xT_lo[:, 4 * b:4 * b + 4, tok(t)], src,
                                      xT_hi[:, 4 * b:4 * b + 4, tok(t)].bitcast(F32), ALU.subtract).then_inc(xT_lo_ok, 1)

            for t in range(NT + 1):
                if t < NT:
                    dve.wait_ge(ld_x[t], 16)
                    if t >= 2:
                        dve.wait_ge(x_tr, 2 * (t - 1))
                    square_sum(ssq[0:rows[t], 0, t:t + 1], x_sb[0:rows[t], t, :], xn[t % 2][0:rows[t], :]).then_inc(ssq1_ok, 1)
                if t >= 1:
                    norm_x(t - 1)
                    if t >= 2:
                        x_lo(t - 2)
            x_lo(NT - 1)
            split_lo(0)
            split_lo(1)

            for b, name in enumerate(BLOCKS):
                split_lo(2 * b + 2)
                for t in range(NT):
                    p = rows[t]
                    if name == "gv":
                        dve.wait_ge(gv_gelu, t + 1)
                        square_sum(ssq[0:p, 1, t:t + 1], gvn[0:p, t, :], sqt[0][0:p, :]).then_inc(gv_ssq, 1)
                        if t == 0:
                            dve.wait_ge(ld_gvb, 16)
                        dve.wait_ge(gv_rstd, t + 1)
                        dve.scalar_tensor_tensor(out=gvn[0:p, t, :], in0=gvn[0:p, t, :], scalar=rstd[0:p, 1, t:t + 1],
                                                 in1=gvb[0:p, :], op0=ALU.mult, op1=ALU.mult).then_inc(gvn_ok, 1)
                    elif name == "u":
                        dve.wait_ge(acc_free[t], 1)
                        dve.wait_ge(mixed, t + 1)
                        if t == 0:
                            dve.wait_ge(ld_bs, 16)
                        if t == NT - 1:
                            dve.wait_ge(st_out, 16)
                        for g in range(GROUPS):
                            c = slice(g * P, (g + 1) * P)
                            ins = dve.scalar_tensor_tensor(out=gvn[0:p, t, c], in0=bank[7][0:p, c], scalar=bs_col[0:p, g:g + 1],
                                                           in1=ut[t % 2][0:p, c], op0=ALU.add, op1=ALU.mult)
                        ins.then_inc(gm_ok, 1)
                    elif name in ("q", "k"):
                        m = NT * (b - 2) + t
                        dve.wait_ge(sq_ok, m + 1)
                        dve.tensor_reduce(ssq8[0:p, m, :], sqt[m % 2][0:p, :].rearrange("p (h d) -> p h d", h=HEADS), AX.X,
                                          ALU.add).then_inc(ssq8_ok, 1)
                        dve.wait_ge(rstd8_ok, m + 1)
                        if m >= 2:
                            dve.wait_ge(qk_tr, m - 1)
                        if m >= NT + 2:
                            dve.wait_ge(k_out[m % 2], 16 * sum(x % 2 == m % 2 for x in range(NT, m)))
                        rb = rstd8[0:p, m, :].rearrange("p (h a) -> p h a", a=1).broadcast_to([p, HEADS, HD])
                        dve.tensor_tensor(qn[m % 2][0:p, :].rearrange("p (h d) -> p h d", h=HEADS),
                                          bank[t][0:p, :].rearrange("p (h d) -> p h d", h=HEADS), rb, ALU.mult)\
                           .then_inc(qk_scaled, 1)
                split_lo(2 * b + 3)

            def abs_z(h):
                dve.wait_ge(z_ok, h + 1)
                if h >= 3:
                    dve.wait_ge(pv_ok, h - 2)
                z = z_sets[h % 2]
                p = P if h < HEADS else DEC
                for dst, src in ((lw[h % 3][:, 0:512], z[0][:, :]), (lw[h % 3][:, 512:1024], z[1][:, :]),
                                 (lw[h % 3][0:p, 1024:ZW], z[2][0:p, 0:256])):
                    ins = dve.tensor_scalar(dst.bitcast(I32), src.bitcast(I32), 0x7FFFFFFF, None, ALU.bitwise_and)
                ins.then_inc(az_ok, 1)

            def softplus(h):
                dve.wait_ge(l_ok, h + 1)
                if h >= 2:
                    dve.wait_ge(rest_ok, h - 1)
                z = z_sets[h % 2]
                s, u = sp[h % 2], later_sums(h)
                if h == HEADS:
                    dve.wait_ge(rest_ok, h)
                    link(dve.memset(s[:, 1024:ZW], 0.0))
                for n, c in enumerate((slice(0, 512), slice(512, 1024), slice(1024, ZW))):
                    p = DEC if h == HEADS and n == 2 else P
                    ins = dve.scalar_tensor_tensor(out=sp[h % 2][0:p, c], in0=z[n][0:p, 0:c.stop - c.start], scalar=0.0,
                                                   in1=lw[h % 3][0:p, c], op0=ALU.max, op1=ALU.add)
                ins.then_inc(sp_ok, 1)
                dve.wait_ge(sp_ok, h + 1)
                n = P if h < HEADS else DW
                if h < HEADS:
                    adds = ((2, s[:, 1152:1280], s[:, 896:1024]), (1, s[:, 768:896], u[:, 2 * P:3 * P]),
                            (0, s[:, 640:768], s[:, 1024:1152]))
                else:
                    adds = ((2, s[:, 768:1024], s[:, 1024:1280]), (1, s[:, 512:768], u[:, 2 * n:3 * n]),
                            (0, s[:, 256:512], u[:, n:2 * n]))
                for k, a, b in adds:
                    ins = dve.tensor_tensor(u[:, k * n:(k + 1) * n], a, b, ALU.add)
                    if k:
                        link(ins)
                ins.then_inc(later_ok, 1)

            def sb_lo(h):
                dve.wait_ge(sbT_hi, h + 1)
                o = turn_bank(PV_USE + h)
                if h < HEADS:
                    r0 = HD * (h % 2)
                    dve.tensor_tensor(xT_lo[r0:r0 + HD, KCH + h // 2, 0:SEQ], o[0:HD, :],
                                      xT_hi[r0:r0 + HD, KCH + h // 2, 0:SEQ].bitcast(F32), ALU.subtract).then_inc(sbT_lo, 1)
                else:
                    for odd in range(2):
                        for a in range(2):
                            r = slice(HD * a, HD * (a + 1))
                            ins = dve.tensor_tensor(xT_lo[r, KCH + odd:KC:2, SEQ:TOK], pairs(o[r, :], odd, a),
                                                    xT_hi[r, KCH + odd:KC:2, SEQ:TOK].bitcast(F32), ALU.subtract)
                    ins.then_inc(sbT_lo, 1)

            for i in range(2):
                dve.wait_ge(k_out[i], K_STORED[i])
            abs_z(0)
            softplus(0)
            for t in range(NT):
                dve.wait_ge(gmT_hi, t + 1)
                src = turn_bank(GM_USE + t)[:, :].rearrange("p (k n) -> p k n", k=KCH)[:, :, 0:rows[t]]
                dve.tensor_tensor(xT_lo[:, 0:KCH, tok(t)], src, xT_hi[:, 0:KCH, tok(t)].bitcast(F32), ALU.subtract)\
                   .then_inc(gmT_lo, 1)
            for h in range(NH):
                if h + 1 < NH:
                    abs_z(h + 1)
                    softplus(h + 1)
                if h >= 1:
                    sb_lo(h - 1)
            sb_lo(NH - 1)

            split_lo(U_IN + 2)
            for t in range(NT):
                p = rows[t]
                dve.wait_ge(proj_done, NT * NB + t + 1)
                dve.tensor_tensor(x_sb[0:p, t, 0:CB], x_sb[0:p, t, 0:CB], bank[t][0:p, :], ALU.add).then_inc(acc_free[t], 1)
            split_lo(U_IN + 3)
            link(dve.memset(lg[:, :, :], 0.0))

            def norm_h(t):
                p = rows[t]
                dve.wait_ge(rstd2_ok, t + 1)
                if t == 0:
                    dve.wait_ge(ld_g2, 16)
                dve.scalar_tensor_tensor(out=xn2[t % 2][0:p, :], in0=x_sb[0:p, t, :], scalar=rstd[0:p, 2, t:t + 1],
                                         in1=g2b[0:p, :], op0=ALU.mult, op1=ALU.mult).then_inc(xn2_ok, 1)

            def logits(t):
                dve.wait_ge(r_mm, t + 1)
                if t == 0:
                    dve.wait_ge(ld_br, 32)
                dve.tensor_tensor(lg[0:rows[t], t, :], bank[7][0:rows[t], 0:NE], br[0:rows[t], :], ALU.add).then_inc(lg_ok, 1)

            for t in range(NT + 2):
                if t < NT:
                    p = rows[t]
                    dve.wait_ge(proj_done, NT * (NB + 1) + t + 1)
                    dve.tensor_tensor(x_sb[0:p, t, CB:D], x_sb[0:p, t, CB:D], bank[t][0:p, :], ALU.add).then_inc(acc_free[t], 1)
                    dve.wait_ge(acc_free[t], 3)
                    if t >= 2:
                        dve.wait_ge(x2_tr, 2 * (t - 1))
                        dve.wait_ge(xn_st[t % 2], 16 * (t // 2))
                    square_sum(ssq[0:p, 2, t:t + 1], x_sb[0:p, t, :], xn2[t % 2][0:p, :]).then_inc(ssq2_ok, 1)
                    norm_h(t)
                if t >= 2:
                    logits(t - 2)

            dve.wait_ge(lg_ok, NT)
            dve.wait_ge(pc, PC_R)
            G4, E4 = lg[:, :, 0:NG], lg[:, :, NG:NE].rearrange("p t (g e) -> p t g e", g=NG)

            def wide(a, n):
                return a[:, :].rearrange("p (t a) -> p t a", a=1).broadcast_to([P, NT, n])

            prio_b = prio[:, :].rearrange("p (a e) -> p a e", a=1).broadcast_to([P, NT, EPG])

            def first_max(dst, values, top, tmp, tmp1):
                link(dve.tensor_reduce(top[:, :], values, AX.X, ALU.max))
                link(dve.tensor_tensor(tmp[:, :, :], values, wide(top, EPG), ALU.is_equal))
                link(dve.tensor_tensor(tmp[:, :, :], tmp[:, :, :], prio_b, ALU.mult))
                link(dve.tensor_reduce(tmp1[:, :], tmp[:, :, :], AX.X, ALU.max))
                link(dve.tensor_tensor(dst[:, :, :], tmp[:, :, :], wide(tmp1, EPG), ALU.is_equal))

            goh, eoh = r4[2], (r4[3], r4[4])
            first_max(goh, G4, r1[0], r4[5], r1[1])
            dve.tensor_tensor(r4[0][:, :, :], G4, wide(r1[0], NG), ALU.subtract).then_inc(rx, 1)
            gb = goh[:, :, :].rearrange("p t (g a) -> p t g a", a=1).broadcast_to([P, NT, NG, EPG])
            link(dve.tensor_tensor(r16[:, :, :, :], E4, gb, ALU.mult))
            le = r4[5]
            link(dve.tensor_reduce(le[:, :, :], r16[:, :, :, :].rearrange("p t g e -> p t e g"), AX.X, ALU.add))
            tmp4 = sel[0][:, :, 0, :]
            link(dve.tensor_copy(r16[:, :, 0, :], le[:, :, :]))
            le1 = r16[:, :, 0, :]
            first_max(eoh[0], le1, r1[2], le, r1[1])
            link(dve.scalar_tensor_tensor(out=r16[:, :, 1, :], in0=eoh[0][:, :, :], scalar=NEG, in1=le1, op0=ALU.mult, op1=ALU.add))
            first_max(eoh[1], r16[:, :, 1, :], r1[3], le, r1[1])
            dve.tensor_tensor(r1[4][:, :], r1[3][:, :], r1[2][:, :], ALU.subtract).then_inc(rx, 1)
            for c in range(2):
                eb = eoh[c][:, :, :].rearrange("p t (a e) -> p t a e", a=1).broadcast_to([P, NT, NG, EPG])
                link(dve.tensor_tensor(sel[c][:, :, :, :], gb, eb, ALU.mult))
            s2 = [s[:, :, :, :].rearrange("p t g e -> p t (g e)") for s in sel]
            s16 = r16[:, :, :, :].rearrange("p t g e -> p t (g e)")
            link(dve.tensor_tensor(s16, s2[0], s2[1], ALU.add))
            dve.tensor_tensor(selb[:, :, :], s16, wide(valid, E), ALU.mult).then_inc(selb_ok, 1)
            for c in range(2):
                for a in range(2):
                    part = tok_part[:, a, :].rearrange("p (t a) -> p t a", a=1).broadcast_to([P, NT, E])
                    dve.tensor_tensor(ids_of[:, c * NT:(c + 1) * NT, a * E:(a + 1) * E], s2[c], part, ALU.mult)
            dve.wait_ge(rank_ok, 1)
            rank = bank[7][:, 0:NT * E].rearrange("p (t e) -> p t e", e=E)
            dve.tensor_tensor(rk16[0][:, :, :], rank, s2[0], ALU.mult)
            link(dve.tensor_tensor(rk16[1][:, :, :], rank, s2[1], ALU.mult))
            dve.tensor_reduce(rank_of[0][:, :], rk16[0][:, :, :], AX.X, ALU.add)
            link(dve.tensor_reduce(rank_of[1][:, :], rk16[1][:, :, :], AX.X, ALU.add))

            def token_slots():
                slots = slot_no[:, :].rearrange("p (a s) -> p a s", a=1).broadcast_to([P, NT, CAP])
                for c in range(2):
                    ins = dve.tensor_tensor(onehot[:, c * NT:(c + 1) * NT, :], slots, wide(rank_of[c], CAP), ALU.is_equal)
                ins.then_inc(onehot_ok, 1)

            def slot_tokens(r):
                dve.wait_ge(ids_mm, r + 1)
                dve.tensor_copy(idx_rows[:, :], bank[4][0:CAP, 0:E]).then_inc(idx_half, 1)
                if not isinstance(r, int):
                    dve.wait_ge(idx_cp, E * r)
                dve.wait_ge(idx_half, r + 1)
                dve.tensor_tensor(idx_all[:, :], idx_rows[:, :], bank[4][0:CAP, E:2 * E], ALU.add).then_inc(idx_ok, 1)

            token_slots()
            link(dve.tensor_reduce(cnt[:, :], bank[7][:, NT * E:NT * E + E], AX.X, ALU.max))
            dve.tensor_scalar(flag[:, :], cnt[:, :], CAP + 0.5, None, ALU.is_gt).then_inc(flag_ok, 1)
            slot_tokens(0)
            dve.wait_ge(r_exp, 2)
            link(dve.tensor_reduce(r1[6][:, :], r4[1][:, :, :], AX.X, ALU.add))
            link(dve.tensor_scalar(r1[7][:, :], r1[5][:, :], 1.0, None, ALU.add))
            link(dve.tensor_tensor(r1[8][:, :], r1[6][:, :], r1[7][:, :], ALU.mult))
            link(dve.reciprocal(gate[0][:, :], r1[8][:, :]))
            dve.tensor_tensor(gate[1][:, :], gate[0][:, :], r1[5][:, :], ALU.mult)
            ids = iota_e[:, :].rearrange("p (a e) -> p a e", a=1).broadcast_to([P, NT, E])
            for c in range(2):
                rk, eid, rd = r1[6 + c], r1[8 + c], r1[10 + c]
                link(dve.tensor_tensor(s16, s2[c], ids, ALU.mult))
                link(dve.tensor_reduce(eid[:, :], s16, AX.X, ALU.add))
                link(dve.tensor_scalar(rd[:, :], rank_of[c][:, :], float(CAP), None, ALU.is_ge))
                for j in range(2, ROUNDS):
                    link(dve.scalar_tensor_tensor(out=rd[:, :], in0=rank_of[c][:, :], scalar=float(j * CAP), in1=rd[:, :],
                                                  op0=ALU.is_ge, op1=ALU.add))
                link(dve.scalar_tensor_tensor(out=rk[:, :], in0=rd[:, :], scalar=-float(CAP), in1=rank_of[c][:, :], op0=ALU.mult,
                                              op1=ALU.add))
                link(dve.scalar_tensor_tensor(out=rk[:, :], in0=eid[:, :], scalar=float(CAP), in1=rk[:, :], op0=ALU.mult, op1=ALU.add))
                ins = dve.scalar_tensor_tensor(out=pos_y[c][:, :], in0=rd[:, :], scalar=float(SLOTS), in1=rk[:, :], op0=ALU.mult,
                                               op1=ALU.add)
            ins.then_inc(places_ok, 1)

            def moe(r):
                s0, u0 = E * r, 3 * E * r

                def lo(m3, slot, unit, n=UNIT):
                    dve.wait_ge(m_hi, unit + 1)
                    dve.tensor_tensor(wlo[SPLIT_OF[m3]][:, 0:n], raw[slot][:, 0:n], whi[SPLIT_OF[m3]][:, 0:n].bitcast(F32),
                                      ALU.subtract).then_inc(m_lo, 1)

                def tokens_lo(i, p):
                    for b in range(2):
                        dve.wait_ge(xsT_hi_ok, 2 * (s0 + i) + b + 1)
                        dve.tensor_tensor(xsT_lo[p][:, 4 * b:4 * b + 4, :].rearrange("p k n -> p (k n)"), bank[5 + b][:, 0:4 * CAP],
                                          xsT_hi[p][:, 4 * b:4 * b + 4, :].rearrange("p k n -> p (k n)").bitcast(F32),
                                          ALU.subtract).then_inc(xsT_lo_ok, 1)

                def times_up(i, p):
                    dve.wait_ge(silu_ok, s0 + i + 1)
                    dve.tensor_tensor(sg[p][:, :], sg[p][:, :], bank[p][0:CAP, FF:CB], ALU.mult).then_inc(a_ok, 1)

                def act_lo(i, p):
                    dve.wait_ge(aT_hi_ok, s0 + i + 1)
                    dve.tensor_tensor(aT_lo[p][:, :, :].rearrange("p k n -> p (k n)"), bank[7][:, 0:2 * CAP],
                                      aT_hi[p][:, :, :].rearrange("p k n -> p (k n)").bitcast(F32), ALU.subtract)\
                       .then_inc(aT_lo_ok, 1)

                def out_rows(i, p, n):
                    dve.wait_ge(m_used, u0 + down_used(i))
                    if not (isinstance(r, int) and isinstance(i, int) and i < 2):
                        dve.wait_ge(y_st[p], 16 * ((E // 2) * r + n))
                    dve.tensor_copy(yout[p][:, CB:D], bank[3][0:CAP, :]).then_inc(y_dve, 1)

                def step(i, j, a):
                    first = isinstance(i, int) and i == 0
                    last = isinstance(i, int) and i == E - 1
                    p = i % 2 if isinstance(i, int) else (3 + a) % 2
                    if not first:
                        lo(1, unit_at(i, 2, j, a)[0], u0 + 3 * i + 1, UNIT // 2)
                        act_lo(i - 1, 1 - p)
                    if not first:
                        lo(2, unit_at(i, 3, j, a)[0], u0 + 3 * i + 2, UNIT // 2 if last else UNIT)
                    if not last:
                        tokens_lo(i + 1, 1 - p)
                    times_up(i, p)
                    if not last:
                        lo(0, unit_at(i, 4, j, a)[0], u0 + 3 * i + 3)
                    if not first:
                        out_rows(i - 1, 1 - p, half_of(i - 1, j, 2 + a))

                if not isinstance(r, int):
                    for c in range(2):
                        ins = dve.tensor_scalar(rank_of[c][:, :], rank_of[c][:, :], -float(CAP), None, ALU.add)
                    ins.then_inc(rank_less, 1)
                    dve.wait_ge(rank_less, r)
                    token_slots()
                    slot_tokens(r)
                dve.wait_ge(m_lo, u0 + 3)
                tokens_lo(0, 0)
                for i in range(3):
                    step(i, 0, 0)
                with dve.Fori(0, (E - 4) // BODY) as j:
                    for a in range(BODY):
                        step(BODY * j + 3 + a, j, a)
                step(E - 1, 0, 0)
                act_lo(E - 1, 1)
                out_rows(E - 1, 1, E // 2 - 1)

            moe(0)
            more = dve.value_load(flag[0:1, 0:1], min_val=0, max_val=1)
            with dve.If(more != 0):
                with dve.Fori(1, ROUNDS) as r:
                    moe(r)

            for t in range(NT):
                p = rows[t]
                dve.wait_ge(yg_ld[t % 2], 32 * (t // 2 + 1))
                for c in range(2):
                    ins = dve.scalar_tensor_tensor(out=x_sb[0:p, t, :], in0=yg[c][t % 2][0:p, :], scalar=gate[c][0:p, t:t + 1],
                                                   in1=x_sb[0:p, t, :], op0=ALU.mult, op1=ALU.add)
                    if c == 0:
                        link(ins)
                ins.then_inc(y_ok, 1)

        @block.tensor
        def _(pe):
            pe.wait_ge(pc, PC_IDENT)
            pe.wait_ge(ws_masked, 1)
            for g in range(GROUPS):
                mm = pe.transpose(bank[7][:, g * P:(g + 1) * P], ws[:, g, :], ident[:, :])
            mm.then_inc(ws_tr, 1)

            def turn4(dst, src, n, done):
                for k in range(4):
                    mm = pe.transpose(dst[:, k * P:k * P + n], src[0:n, k * P:(k + 1) * P], ident[0:n, 0:n])
                mm.then_inc(done, 1)

            for t in range(NT):
                pe.wait_ge(xn_ok, t + 1)
                for b in range(2):
                    wait_turn(pe, X_USE + 2 * t + b)
                    turn4(turn_bank(X_USE + 2 * t + b), xn[t % 2][:, 4 * b * P:(4 * b + 4) * P], rows[t], x_tr)

            def three_passes(acc, x_hi, x_lo, w_hi, w_lo, start, stop):
                pe.matmul(acc, x_hi, w_hi, start=start, stop=False)
                pe.matmul(acc, x_hi, w_lo, start=False, stop=False)
                return pe.matmul(acc, x_lo, w_hi, start=False, stop=stop)

            def project(blk, after):
                for half in range(2):
                    n = 2 * blk + half
                    pe.wait_ge(hi_ok, n + 1)
                    pe.wait_ge(lo_ok, n + 1)
                    for t in range(NT):
                        if blk == 0 and half == 0:
                            pe.wait_ge(xT_lo_ok, 2 * t + 2)
                        if blk >= 1 and half == 0:
                            bank_read(blk - 1, t)
                        for k in range(UK):
                            c = slice(k * CB, (k + 1) * CB)
                            kk = UK * half + k
                            mm = three_passes(bank[t][0:rows[t], :], xT_hi[:, kk, tok(t)], xT_lo[:, kk, tok(t)],
                                              whi[n % 2][:, c], wlo[n % 2][:, c], kk == 0, kk == KC - 1)
                        if half == 1:
                            mm.then_inc(proj_done, 1)
                        elif t == NT - 1:
                            mm.then_inc(half_done, 1)
                        if after[half]:
                            after[half](t)

            def bank_read(blk, t):
                name = BLOCKS[blk] if blk < NB else "out"
                if name == "gv":
                    pe.wait_ge(gv_gelu, t + 1)
                elif name == "u":
                    pe.wait_ge(acc_free[t], 1)
                elif name in ("q", "k"):
                    pe.wait_ge(qk_scaled, NT * (blk - 2) + t + 1)
                elif name == "v":
                    pe.wait_ge(v_ok, t + 1)
                else:
                    pe.wait_ge(acc_free[t], 2)

            def mix_rows(t):
                p = rows[t]
                pe.wait_ge(gvn_ok, t + 1)
                if t == 0:
                    pe.wait_ge(wmT_ok, 1)
                else:
                    pe.wait_ge(gm_ok, t)
                for g in range(GROUPS):
                    c = slice(g * P, (g + 1) * P)
                    mm = pe.matmul(bank[7][0:p, c], WmT[0:p, g, 0:p], gvn[0:p, t, c], start=True, stop=True)
                mm.then_inc(mixed, 1)

            def turn_qk(m):
                t = m % NT
                pe.wait_ge(qk_ok, m + 1)
                wait_turn(pe, QK_USE + m)
                turn4(turn_bank(QK_USE + m), qn[m % 2], rows[t], qk_tr)

            def turn_cache():
                for c in range(NCH):
                    pe.wait_ge(ld_ck[c // 2], 16)
                    wait_turn(pe, CK_USE + c)
                    turn4(turn_bank(CK_USE + c), xn[c // 2][:, (c % 2) * CB:(c % 2 + 1) * CB], P, ck_tr)

            project(0, (None, None))
            turn_cache()
            project(1, (None, mix_rows))
            project(2, (None, None))
            project(3, (lambda t: turn_qk(t), None))
            project(4, (lambda t: turn_qk(NT + t), None))

            def scores(h):
                z = z_sets[h % 2]
                if h == 0:
                    pe.wait_ge(qkT_ok, 2 * NT)
                    pe.wait_ge(pc, PC_MASK)
                    bank_read(NB - 1, 2)
                elif h == 1:
                    bank_read(NB - 1, 4)
                else:
                    pe.wait_ge(w_ok, h - 1)
                if h < HEADS:
                    for bk, c0, n, c, q0 in regions:
                        pe.matmul(z[bk][:, c0:c0 + n], kT[:, h // 2, c * P:(c + 1) * P], qpad[:, h, q0:SEQ],
                                  start=(c0 == 0), stop=True, skip_group_check=True)
                        mm = pe.matmul(z[bk][:, c0:c0 + P], identb[:, :], maskneg[:, :], start=False, stop=True,
                                       skip_group_check=True)
                else:
                    pe.wait_ge(ckT_ok, NCH)
                    for bk, c0, n, c in s_regions:
                        kt, p = (ckT[:, :, c * P:(c + 1) * P], P) if c < NCH else (kT[:, :, SEQ:TOK], DEC)
                        for j in range(KCH):
                            w0 = c0 + j // 2 * P
                            pe.matmul(z[bk][0:p, w0:w0 + P], kt[:, j, :], qs[:, j * P:(j + 1) * P],
                                      start=(c0 == 0 and j == 0), stop=True, skip_group_check=True)
                    mm = pe.matmul(z[bk][0:DEC, c0:c0 + n], identb[0:DEC, 0:DEC], maskneg8[:, :, :].rearrange("p h n -> p (h n)"),
                                   start=False, stop=True, skip_group_check=True)
                mm.then_inc(z_ok, 1)

            def suffix_sums(h):
                z, s = z_sets[h % 2], sp[h % 2]
                pe.wait_ge(sp_ok, h + 1)
                pe.wait_ge(pc, PC_U)
                u = later_sums(h)
                for bk, c0, n, c, *_ in (regions if h < HEADS else s_regions):
                    p = P if h < HEADS or c < NCH else DEC
                    pe.matmul(z[bk][0:p, c0:c0 + n], negU[0:p, 0:p], s[0:p, 512 * bk + c0:512 * bk + c0 + n],
                              start=False, stop=True, skip_group_check=True)
                pe.wait_ge(later_ok, h + 1)
                if h < HEADS:
                    rest = ((0, P, s[:, 512:512 + P]), (0, 2 * P, u[:, 0:2 * P]), (1, P, s[:, 1024:1024 + P]),
                            (1, 2 * P, u[:, 2 * P:3 * P]), (2, P, s[:, 896:1024]))
                else:
                    rest = ((0, 0, u[:, 0:DW]), (0, DW, u[:, DW:2 * DW]), (1, 0, u[:, 2 * DW:3 * DW]),
                            (1, DW, s[:, 1024:1024 + DW]))
                for bk, c0, a in rest:
                    mm = pe.matmul(z[bk][:, c0:c0 + a.shape[-1]], negones[:, :], a, start=False, stop=True,
                                   skip_group_check=True)
                mm.then_inc(rest_ok, 1)

            def values(h):
                w = lw[h % 3]
                o = turn_bank(PV_USE + h)
                pe.wait_ge(w_ok, h + 1)
                wait_turn(pe, PV_USE + h)
                if h == 0:
                    pe.wait_ge(v_ok, NT)
                if h < HEADS:
                    for bk, c0, n, c, q0 in sorted(regions, key=lambda x: x[3]):
                        mm = pe.matmul(o[0:HD, q0:SEQ], v_sb[:, c, h * HD:(h + 1) * HD], w[:, 512 * bk + c0:512 * bk + c0 + n],
                                       start=(c == 0), stop=True, skip_group_check=True)
                else:
                    pe.wait_ge(ld_cv, 16)
                    for j in range(KCH):
                        hc = slice(j * P, (j + 1) * P)
                        for bk, c0, n, c in s_regions:
                            v, p = (cv[:, c, hc], P) if c < NCH else (v_sb[0:DEC, NT - 1, hc], DEC)
                            w0 = 512 * bk + c0 + j // 2 * P
                            mm = pe.matmul(o[:, hc], v, w[0:p, w0:w0 + P], start=(j == 0 and c == 0), stop=True,
                                           skip_group_check=True)
                mm.then_inc(pv_ok, 1)

            scores(0)
            for t in range(NT):
                pe.wait_ge(gm_ok, t + 1)
                wait_turn(pe, GM_USE + t)
                turn4(turn_bank(GM_USE + t), gvn[:, t, :], rows[t], gm_tr)
            for h in range(NH):
                if h + 1 < NH:
                    scores(h + 1)
                suffix_sums(h)
                if h >= 1:
                    values(h - 1)
            values(NH - 1)

            pe.wait_ge(w_ok, NH)
            pe.wait_ge(gmT_lo, NT)
            pe.wait_ge(sbT_lo, NH)
            project(NB, (None, None))

            def router(t):
                pe.wait_ge(x2T_ok, 2 * t + 2)
                if t == 0:
                    pe.wait_ge(wr_padded, 1)
                else:
                    pe.wait_ge(lg_ok, t)
                for k in range(KC):
                    mm = pe.matmul(bank[7][0:rows[t], 0:P], x2T[:, k, 0:rows[t]], wr_pad[:, k, :], start=(k == 0), stop=(k == KC - 1))
                mm.then_inc(r_mm, 1)

            project(NB + 1, (None, None))
            for t in range(NT):
                pe.wait_ge(xn2_ok, t + 1)
                for b in range(2):
                    if t >= 1:
                        pe.wait_ge(x2T_ok, 2 * t - 1 + b)
                    turn4(bank[5 + b], xn2[t % 2][:, 4 * b * P:(4 * b + 4) * P], rows[t], x2_tr)
                router(t)
            pe.wait_ge(selb_ok, 1)
            pe.wait_ge(lg_ok, NT)
            for t in range(NT):
                dst = bank[7][:, t * E:(t + 1) * E]
                for t2 in range(t):
                    pe.matmul(dst, onesb[:, :], selb[:, t2, :], start=(t2 == 0), stop=False)
                pe.matmul(dst, before[:, :], selb[:, t, :], start=(t == 0), stop=True)
            for t in range(NT):
                mm = pe.matmul(bank[7][:, NT * E:(NT + 1) * E], onesb[:, :], selb[:, t, :], start=(t == 0), stop=(t == NT - 1))
            mm.then_inc(rank_ok, 1)

            def slot_table(r):
                pe.wait_ge(onehot_ok, r + 1)
                for m in range(2 * NT):
                    mm = pe.matmul(bank[4][0:CAP, 0:2 * E], onehot[:, m, :], ids_of[:, m, :], start=(m == 0), stop=(m == 2 * NT - 1))
                mm.then_inc(ids_mm, 1)

            def moe(r):
                s0, u0 = E * r, 3 * E * r
                slot_table(r)

                def turn_tokens(i, p, n):
                    s = s0 + i
                    pe.wait_ge(xs_ld[p], 16 * ((E // 2) * r + n + 1))
                    for b in range(2):
                        if not (isinstance(s, int) and s < 1):
                            pe.wait_ge(xsT_lo_ok, 2 * s - 1 + b)
                        for k in range(4):
                            mm = pe.transpose(bank[5 + b][:, k * CAP:(k + 1) * CAP],
                                              xs[p][:, (4 * b + k) * P:(4 * b + k + 1) * P], ident[0:CAP, 0:CAP])
                        mm.then_inc(xs_tr, 1)

                def gate_up(i, p, half, m3, unit):
                    s = s0 + i
                    if half == 0:
                        pe.wait_ge(xsT_lo_ok, 2 * s + 2)
                        if isinstance(s, int) and s < 2:
                            pe.wait_ge(acc_free[s], 3)
                        else:
                            pe.wait_ge(a_ok, s - 1)
                    pe.wait_ge(m_lo, unit + 1)
                    for k in range(UK):
                        c = slice(k * CB, (k + 1) * CB)
                        kk = UK * half + k
                        mm = three_passes(bank[p][0:CAP, :], xsT_hi[p][:, kk, :], xsT_lo[p][:, kk, :],
                                          whi[SPLIT_OF[m3]][:, c], wlo[SPLIT_OF[m3]][:, c], kk == 0, kk == KC - 1)
                    mm.then_inc(m_used, 1)

                def turn_act(i, p):
                    s = s0 + i
                    pe.wait_ge(a_ok, s + 1)
                    if not (isinstance(s, int) and s < 1):
                        pe.wait_ge(aT_lo_ok, s)
                    for k in range(2):
                        mm = pe.transpose(bank[7][:, k * CAP:(k + 1) * CAP], sg[p][:, k * P:(k + 1) * P], ident[0:CAP, 0:CAP])
                    mm.then_inc(a_tr, 1)

                def down(i, p, m3, unit):
                    s = s0 + i
                    pe.wait_ge(aT_lo_ok, s + 1)
                    pe.wait_ge(m_lo, unit + 1)
                    pe.wait_ge(m_lo_pool, (E + 1) * r + i + 2)
                    if isinstance(s, int) and s < 1:
                        pe.wait_ge(acc_free[2], 3)
                        pe.wait_ge(acc_free[3], 3)
                    else:
                        pe.wait_ge(y_act, s)
                        pe.wait_ge(y_dve, s)
                    for n in range(2):
                        for k in range(2):
                            c = slice(k * D + n * CB, k * D + (n + 1) * CB)
                            mm = three_passes(bank[2 + n][0:CAP, :], aT_hi[p][:, k, :], aT_lo[p][:, k, :],
                                              whi[SPLIT_OF[m3]][:, c], wlo[SPLIT_OF[m3]][:, c], k == 0, k == 1)
                    mm.then_inc(m_used, 1)

                def step(i, j, a):
                    p = i % 2 if isinstance(i, int) else (3 + a) % 2
                    first = isinstance(i, int) and i == 0
                    last = isinstance(i, int) and i == E - 1
                    gate_up(i, p, 0, 0 if first else 2, u0 + (0 if first else 3 * i - 1))
                    if first:
                        turn_tokens(1, 1, 0)
                    else:
                        turn_act(i - 1, 1 - p)
                    gate_up(i, p, 1, 1 if first else 0, u0 + (1 if first else 3 * i))
                    if not first and not last:
                        turn_tokens(i + 1, 1 - p, half_of(i + 1, j, 4 + a))
                    if not first:
                        down(i - 1, 1 - p, 1, u0 + 3 * i + 1)

                turn_tokens(0, 0, 0)
                for i in range(3):
                    step(i, 0, 0)
                with pe.Fori(0, (E - 4) // BODY) as j:
                    for a in range(BODY):
                        step(BODY * j + 3 + a, j, a)
                step(E - 1, 0, 0)
                turn_act(E - 1, 1)
                down(E - 1, 1, 2, u0 + 3 * E - 1)

            moe(0)
            pe.wait_ge(flag_ok, 1)
            more = pe.value_load(flag[0:1, 0:1], min_val=0, max_val=1)
            with pe.If(more != 0):
                with pe.Fori(1, ROUNDS) as r:
                    moe(r)


_INS = ["x_prompt", "x_sample", "cache_sb_k", "cache_sb_v", "norm1_g", "w_in", "gm_v_norm_g", "gm_w_s", "gm_b_s",
        "q_norm_g", "k_norm_g", "w_out", "norm2_g", "w_router_group", "b_router_group", "w_router_expert",
        "b_router_expert", "w_gate", "w_up", "w_down"]


def kernel(**inputs):
    import numpy as _np
    import concourse.bacc as _bacc
    from concourse import mybir as _mybir
    from concourse.bass_utils import run_bass_kernel_spmd as _run

    nc = _bacc.Bacc("TRN2", target_bir_lowering=False, num_devices=1)
    arrays, args = {}, []
    for name in _INS:
        a = _np.ascontiguousarray(inputs[name])
        arrays[f"in_{name}_dram"] = a
        args.append(nc.dram_tensor(f"in_{name}_dram", a.shape, _mybir.dt.from_np(a.dtype), kind="ExternalInput").ap())
    xp, xs, ck = inputs["x_prompt"].shape, inputs["x_sample"].shape, inputs["cache_sb_k"].shape
    groups = inputs["gm_w_s"].shape[1]
    outs = [xp, xs] + [(1, *xp[:2], *ck[3:])] * 2 + [(1, *xs[:2], *ck[3:])] * 2
    outs.append((1, *xs[:2], groups, inputs["gm_v_norm_g"].shape[1] // groups))
    for i, shape in enumerate(outs):
        args.append(nc.dram_tensor(f"out_{i}_dram", shape, _mybir.dt.float32, kind="ExternalOutput").ap())
    trunk_step(nc, *args)
    r = _run(nc, [arrays], core_ids=[0])
    return tuple(r.results[0][f"out_{i}_dram"] for i in range(len(outs)))
```

```python
from contextlib import ExitStack

import concourse.bass as bass
from concourse import mybir
from concourse.alu_op_type import AluOpType as ALU

ACT = mybir.ActivationFunctionType
AX = mybir.AxisListType
F32 = mybir.dt.float32
F32R = mybir.dt.float32r
BF16 = mybir.dt.bfloat16
I32 = mybir.dt.int32
P = 128
EPS = 1e-6
NEG = -1e30


def trunk_step(nc, x_prompt, x_sample, cache_k, cache_v, norm1_g, w_in, gm_v_norm_g, gm_w_s, gm_b_s,
               q_norm_g, k_norm_g, w_out, norm2_g, w_rg, b_rg, w_re, b_re, w_gate, w_up, w_down,
               y_prompt, y_sample, k_prompt, v_prompt, k_sample, v_sample, gv_sample):
    SEQ, D = x_prompt.shape[1], x_prompt.shape[2]
    DEC = x_sample.shape[1]
    HEADS, HD = cache_k.shape[3], cache_k.shape[4]
    GROUPS = gm_w_s.shape[1]
    NG, EPG = w_re.shape[1], w_re.shape[3]
    E, FF = w_gate.shape[1], w_gate.shape[3]
    KC = D // P
    NT = SEQ // P + 1
    TOK = SEQ + DEC
    rows = [P] * (NT - 1) + [DEC]
    CB = 512
    UK = 4
    UNIT = UK * CB
    BLOCKS = ("gv", "u", "q", "k", "v")
    block_col = {"u": 0, "gv": CB, "q": 2 * CB, "k": 3 * CB, "v": 4 * CB}
    NB = len(BLOCKS)
    U_IN = 2 * NB
    U_ALL = U_IN + 2 * (D // CB)
    NCH = SEQ // P
    KCH = CB // P
    NE = NG + E
    CAP = 96
    ROUNDS = -(-TOK // CAP)
    SLOTS = E * CAP
    NRAW = 12
    BODY = 4
    AHEAD = 2
    assert FF * 2 == CB and D == 2 * CB and HEADS * HD == CB and SEQ == CB and E == 16

    xn_dram = nc.dram_tensor("normed_tokens", [TOK, D], F32, kind="Internal").ap()
    y_dram = nc.dram_tensor("expert_rows", [ROUNDS * SLOTS, D], F32, kind="Internal").ap()

    with ExitStack() as ctx:
        def sb(name, shape, dt=F32, stack=ctx):
            return stack.enter_context(nc.sbuf_tensor(name, shape, dt))

        def sem(name):
            return ctx.enter_context(nc.semaphore(name))

        bank = [ctx.enter_context(nc.psum_tensor(f"bank{i}", [P, 512], F32)) for i in range(8)]

        raw = [sb(f"raw{i}", [P, UNIT]) for i in range(3)]
        whi = [sb(f"whi{i}", [P, UNIT], F32R) for i in range(2)]
        wlo = [sb(f"wlo{i}", [P, UNIT], F32R) for i in range(2)]
        x_sb = sb("x_sb", [P, NT, D])
        xT_s = sb("xT_s", [P, KC, DEC])
        ident = sb("ident", [P, P])
        identb = sb("identb", [P, P], BF16)
        maskneg = sb("maskneg", [P, P], BF16)
        maskneg8 = sb("maskneg8", [DEC, HEADS, DEC], BF16)
        negU = sb("negU", [P, P])
        negones = sb("negones", [P, P])
        before = sb("before", [P, P], BF16)
        onesb = sb("onesb", [P, P], BF16)
        ssq = sb("ssq", [P, 4, NT])
        rstd = sb("rstd", [P, 3, NT])
        ssq8 = sb("ssq8", [P, 2 * NT, HEADS])
        rstd8 = sb("rstd8", [P, 2 * NT, HEADS])
        mhalf = sb("mhalf", [P, HEADS])
        bs_col = sb("bs_col", [P, GROUPS])
        qg = sb("qg", [P, HD])
        kg = sb("kg", [P, HD])
        wr = sb("wr", [P, KC, NE])
        br = sb("br", [P, NE])
        tok_part = sb("tok_part", [P, 2, NT])
        valid = sb("valid", [P, NT])
        iota_i = sb("iota_i", [P, CAP], I32)
        slot_no = sb("slot_no", [P, CAP], BF16)
        iota_e = sb("iota_e", [P, E])
        prio = sb("prio", [P, EPG])
        lg = sb("lg", [P, NT, NE])
        r1 = [sb(f"r1_{i}", [P, NT]) for i in range(12)]
        selb = sb("selb", [P, NT, E], BF16)
        gate = [sb(f"gate{i}", [P, NT]) for i in range(2)]
        rank_of = [sb(f"rank_of{i}", [P, NT]) for i in range(2)]
        pos_y = [sb(f"pos_y{i}", [P, NT], I32) for i in range(2)]
        cnt = sb("cnt", [P, 1])
        flag = sb("flag", [P, 1], I32)
        idx_all = sb("idx_all", [CAP, E], I32)
        idx_cur = [sb(f"idx_cur{i}", [CAP, 1], I32) for i in range(2)]

        mix = ExitStack()
        xT_hi = sb("xT_hi", [P, KC, SEQ], F32R, stack=mix)
        xT_lo = sb("xT_lo", [P, KC, SEQ], F32R, stack=mix)
        qpad = sb("qpad", [P, HEADS, SEQ], stack=mix)
        qs = sb("qs", [P, KCH * P], stack=mix)
        kT = sb("kT", [P, KCH, TOK], stack=mix)
        v_sb = sb("v_sb", [P, NT, CB], stack=mix)
        gvn = sb("gvn", [P, NT, CB], stack=mix)
        ckT = sb("ckT", [P, KCH, SEQ], stack=mix)
        cv = sb("cv", [P, NCH, CB], stack=mix)
        ws = ckT[:, :, 0:P]
        st_a = ExitStack()
        xn = [sb(f"xn{i}", [P, D], stack=st_a) for i in range(2)]
        g1b = sb("g1b", [P, D], stack=st_a)
        sqt = [sb(f"sqt{i}", [P, CB], stack=st_a) for i in range(2)]
        gvb = sb("gvb", [P, CB], stack=st_a)
        WmT = sb("WmT", [P, GROUPS, P], stack=st_a)
        qn = [sb(f"qn{i}", [P, CB], stack=st_a) for i in range(2)]
        ut = qn
        st_a.close()
        st_b = ExitStack()
        ZW = 1280
        lw = [sb(f"lw{i}", [P, ZW], stack=st_b)[:, :] for i in range(3)]
        lw += [x_[:, :, :].rearrange("p c n -> p (c n)")[:, 0:ZW] for x_ in (ckT, cv)]
        sp = [sb(f"sp{i}", [P, ZW], stack=st_b) for i in range(2)]
        later = sb("later", [P, 6 * P], stack=st_b)
        st_b.close()
        st_c = ExitStack()
        sb("gap_c", [P, 512], stack=st_c)
        xn2 = [sb(f"xn2_{i}", [P, D], stack=st_c) for i in range(2)]
        g2b = sb("g2b", [P, D], stack=st_c)
        x2T = sb("x2T", [P, KC, P], stack=st_c)
        wr_pad = sb("wr_pad", [P, KC, P], stack=st_c)
        rk16 = [sb(f"rk16_{i}", [P, NT, E], stack=st_c) for i in range(2)]
        r4 = [sb(f"r4_{i}", [P, NT, EPG], stack=st_c) for i in range(6)]
        r16 = sb("r16", [P, NT, NG, EPG], stack=st_c)
        sel = [sb(f"sel{i}", [P, NT, NG, EPG], stack=st_c) for i in range(2)]
        st_c.close()
        mix.close()
        st_l = ExitStack()
        x2T_late = sb("x2T_late", [P, KC, P], stack=st_l)
        xn2_late = sb("xn2_late", [P, D], stack=st_l)
        st_l.close()
        yout = [sb(f"yout{i}", [CAP, D]) for i in range(2)]
        late = [sb(f"raw{i}", [P, UNIT]) for i in range(9, NRAW)]
        eraw = [sb(f"raw{i}", [P, UNIT]) for i in range(3, 9)] + [raw[2], raw[0]] + late + [raw[1]]
        whi.append(sb("whi2", [P, UNIT], F32R))
        wlo.append(sb("wlo2", [P, UNIT], F32R))
        xs = [sb(f"xs{i}", [CAP, D]) for i in range(2)]
        xsT_hi = [sb(f"xsT_hi{i}", [P, KC, CAP], F32R) for i in range(2)]
        xsT_lo = [sb(f"xsT_lo{i}", [P, KC, CAP], F32R) for i in range(2)]
        sg = [sb(f"sg{i}", [CAP, FF]) for i in range(2)]
        aT_hi = [sb(f"aT_hi{i}", [P, 2, CAP], F32R) for i in range(2)]
        aT_lo = [sb(f"aT_lo{i}", [P, 2, CAP], F32R) for i in range(2)]
        ids_of = sb("ids_of", [P, 2 * NT, 2 * E], BF16)
        onehot = sb("onehot", [P, 2 * NT, CAP], BF16)
        idx_rows = sb("idx_rows", [CAP, E])
        yg = [[eraw[t][:, c * D:(c + 1) * D] for t in range(NT)] for c in range(2)]

        xn2_of = [xn2[t % 2][:, :] for t in range(NT - 1)] + [xn2_late[:, :]]
        x2T_of = [x2T[:, :, :]] * NT
        x2T_of[NT - 2] = x2T_late[:, :, :]
        xn2_tiles = [[t for t in range(NT - 1) if t % 2 == i] for i in range(2)] + [[NT - 1]]

        ld_x = [sem(f"ld_x{t}") for t in range(NT)]
        ld_raw = [sem(f"ld_raw{i}") for i in range(3)]
        ld_g1, ld_ws, ld_gvb, ld_bs = sem("ld_g1"), sem("ld_ws"), sem("ld_gvb"), sem("ld_bs")
        ld_qg, ld_kg, ld_wr, ld_br = sem("ld_qg"), sem("ld_kg"), sem("ld_wr"), sem("ld_br")
        ld_ck = [sem(f"ld_ck{i}") for i in range(2)]
        ld_cv, ld_g2 = sem("ld_cv"), sem("ld_g2")
        pc = sem("pool_const")
        ws_masked = sem("ws_masked")
        ws_tr, wmT_ok = sem("ws_tr"), sem("wmT_ok")
        wr_padded = sem("wr_padded")
        ssq1_ok, rstd1_ok, xn_ok = sem("ssq1_ok"), sem("rstd1_ok"), sem("xn_ok")
        x_tr, xT_hi_ok, xT_lo_ok = sem("x_tr"), sem("xT_hi_ok"), sem("xT_lo_ok")
        ck_tr, ckT_ok = sem("ck_tr"), sem("ckT_ok")
        hi_ok, lo_ok = sem("hi_ok"), sem("lo_ok")
        half_done, proj_done = sem("half_done"), sem("proj_done")
        acc_free = [sem(f"acc_free{t}") for t in range(NT)]
        gv_gelu, gv_ssq, gv_rstd, gvn_ok = sem("gv_gelu"), sem("gv_ssq"), sem("gv_rstd"), sem("gvn_ok")
        u_gelu, mixed, gm_ok = sem("u_gelu"), sem("mixed"), sem("gm_ok")
        sq_ok, ssq8_ok, rstd8_ok = sem("sq_ok"), sem("ssq8_ok"), sem("rstd8_ok")
        qk_scaled, qk_ok, qk_tr, qkT_ok = sem("qk_scaled"), sem("qk_ok"), sem("qk_tr"), sem("qkT_ok")
        v_ok = sem("v_ok")
        k_out = [sem(f"k_out{i}") for i in range(2)]
        st_out, v_out = sem("st_out"), sem("v_out")
        gm_tr, gmT_hi, gmT_lo = sem("gm_tr"), sem("gmT_hi"), sem("gmT_lo")
        z_ok, az_ok, e_ok, l_ok, sp_ok = sem("z_ok"), sem("az_ok"), sem("e_ok"), sem("l_ok"), sem("sp_ok")
        later_ok = sem("later_ok")
        rest_ok, w_ok, pv_ok, sbT_hi, sbT_lo = sem("rest_ok"), sem("w_ok"), sem("pv_ok"), sem("sbT_hi"), sem("sbT_lo")
        h_ok, ssq2_ok, rstd2_ok, xn2_ok = sem("h_ok"), sem("ssq2_ok"), sem("rstd2_ok"), sem("xn2_ok")
        xn_st = [sem(f"xn_st{i}") for i in range(3)]
        x2_tr, x2T_ok, r_mm, lg_ok = sem("x2_tr"), sem("x2T_ok"), sem("r_mm"), sem("lg_ok")
        rx, r_exp = sem("router_to_act"), sem("router_exp")
        selb_ok, rank_ok, flag_ok = sem("selb_ok"), sem("rank_ok"), sem("flag_ok")
        rank_less, onehot_ok, ids_mm = sem("rank_less"), sem("onehot_ok"), sem("ids_mm")
        idx_half, idx_ok, idx_cp, places_ok = sem("idx_half"), sem("idx_ok"), sem("idx_cp"), sem("places_ok")
        m_ld = [sem(f"m_ld{i}") for i in range(NRAW)]
        m_hi, m_lo, m_lo_pool, m_used = sem("m_hi"), sem("m_lo"), sem("m_lo_pool"), sem("m_used")
        xs_ld = [sem(f"xs_ld{i}") for i in range(2)]
        xs_tr, xsT_hi_ok, xsT_lo_ok = sem("xs_tr"), sem("xsT_hi_ok"), sem("xsT_lo_ok")
        silu_ok, a_ok, a_tr, aT_hi_ok, aT_lo_ok = (sem(n) for n in ("silu_ok", "a_ok", "a_tr", "aT_hi_ok", "aT_lo_ok"))
        y_act, y_dve = sem("y_act"), sem("y_dve")
        y_st = [sem(f"y_st{i}") for i in range(2)]
        yg_ld = [sem(f"yg_ld{t}") for t in range(NT)]
        y_ok, y_out = sem("y_ok"), sem("y_out")
        dch, pch = sem("dve_chain"), sem("pool_chain")
        pool_tick, sp_tick = sem("pool_tick"), sem("sp_tick")

        def tok(t):
            return slice(t * P, t * P + rows[t])

        X_USE, CK_USE = 0, 2 * NT
        QK_USE = CK_USE + NCH

        def block_parts(t):
            if t < NT - 1:
                return [(bank[t][:, :], slice(0, CB))]
            return [(bank[t][j * DEC:(j + 1) * DEC, 0:P], slice(j * P, (j + 1) * P)) for j in range(CB // P)]

        def turn_bank(use):
            return bank[5 + use % 2]

        def wait_turn(pe, use):
            u = use - 2
            if u < 0:
                return
            if u < CK_USE:
                pe.wait_ge(xT_lo_ok, u + 1)
            elif u < QK_USE:
                pe.wait_ge(ckT_ok, u - CK_USE + 1)
            else:
                pe.wait_ge(qkT_ok, u - QK_USE + 1)

        def z_of(h):
            if h == 0:
                return [bank[5], bank[6], bank[7]]
            return [bank[0], bank[1], bank[2]] if h % 2 else [bank[3], bank[4], bank[7]]

        regions = [(0, 0, 512, 0, 0), (1, 0, 384, 1, 128), (1, 384, 128, 3, 384), (2, 0, 256, 2, 256)]
        DW = HEADS * DEC
        s_regions = [(c * DW // 512, c * DW % 512, DW, c) for c in range(NCH + 1)]
        NH = HEADS + 1
        NV = 1 + HEADS // 2

        def parts_of(h, a):
            p = P if h else DEC
            return [(0, P, slice(0, 512))] if a == 0 else [(1, P, slice(512, 1024)), (2, p, slice(1024, ZW))]

        def later_sums(h):
            return later[:, 3 * P * (h % 2):3 * P * (h % 2 + 1)] if h else later[:, :]

        def pairs(a, odd, side):
            c = odd * (P + 2 * DEC) + side * DEC
            return a.rearrange("p (w c) -> p w c", c=2 * P)[:, :, c:c + DEC]

        SPLIT_OF = (0, 2, 1)

        def unit_at(i, c, j, a):
            m = 3 * i - 1 + c if isinstance(i, int) else 3 * (3 + a) - 1 + c
            return m % NRAW, (0 if isinstance(i, int) else j) + m // NRAW

        def half_of(i, j, a):
            return i // 2 if isinstance(i, int) else 2 * j + a // 2

        def gate_up_used(i):
            return 2 if isinstance(i, int) and i == 0 else 3 * i + 1

        def down_used(i):
            return 3 * E if isinstance(i, int) and i == E - 1 else 3 * i + 5

        K_STORED = [16 * sum(m % 2 == i for m in range(NT, 2 * NT)) for i in range(2)]
        PC_IDENT, PC_MASK, PC_U, PC_QPAD, PC_R = 1, 2, 3, 5, 6

        def unit_used(eng, n):
            if n % 2 == 0:
                eng.wait_ge(half_done, n // 2 + 1)
            else:
                eng.wait_ge(proj_done, NT * (n // 2 + 1))

        block = ctx.enter_context(nc.Block())

        @block.sync
        def _(sp_):
            def load_x(t):
                src = x_prompt[0, tok(t), :] if t < NT - 1 else x_sample[0, :, :]
                sp_.dma_start(x_sb[0:rows[t], t, :], src).then_inc(ld_x[t], 16)

            def load_unit(n):
                if n >= 3:
                    unit_used(sp_, n - 3)
                if n < U_IN:
                    src, c0, half = w_in, block_col[BLOCKS[n // 2]], n % 2
                else:
                    src, c0, half = w_out, CB * ((n - U_IN) // 2), n % 2
                view = src[0, half * UK * P:(half + 1) * UK * P, c0:c0 + CB].rearrange("(k p) n -> p k n", p=P)
                sp_.dma_start(raw[n % 3][:, :].rearrange("p (k n) -> p k n", k=UK), view).then_inc(ld_raw[n % 3], 16)

            load_x(0)
            load_x(1)
            load_unit(0)
            load_x(2)
            load_unit(1)
            for t in range(3, NT):
                load_x(t)
            for n in range(2, U_ALL):
                load_unit(n)

            def load_gate_up(e, half, slot):
                dst = eraw[slot][:, :].rearrange("p (k n) -> p k n", k=UK)
                for j, w in enumerate((w_gate, w_up)):
                    src = w[0, e, half * UK * P:(half + 1) * UK * P, :].rearrange("(k p) f -> p k f", p=P)
                    sp_.dma_start(dst[:, :, j * FF:(j + 1) * FF], src).then_inc(m_ld[slot], 16)

            def load_down(e, slot):
                for k in range(2):
                    sp_.dma_start(eraw[slot][:, k * D:(k + 1) * D], w_down[0, e, k * P:(k + 1) * P, :])\
                       .then_inc(m_ld[slot], 16)

            def moe_loads(r):
                u0 = 3 * E * r

                def raw_free(m):
                    if isinstance(r, int) and isinstance(m, int) and m < NRAW:
                        if m < 6:
                            sp_.wait_ge(pv_ok, NV)
                            sp_.wait_ge(gmT_lo, NT)
                            sp_.wait_ge(st_out, 16)
                            sp_.wait_ge(v_out, 16 * NT)
                        else:
                            unit_used(sp_, U_ALL - 3 + min(m - 6, 2))
                    else:
                        n = u0 + m - (NRAW - 1)
                        sp_.wait_ge(m_hi, n)
                        sp_.wait_ge(m_lo, n)
                        sp_.sem_inc(sp_tick, 1)

                def gate_up_unit(i, half, m, slot):
                    raw_free(m)
                    load_gate_up(i, half, slot)

                def down_unit(i, m, slot):
                    raw_free(m)
                    load_down(i, slot)

                def first(m):
                    i = (m + 1) // 3
                    if not isinstance(r, int):
                        if m % 3 == 1:
                            sp_.wait_ge(m_lo_pool, (E + 1) * r - 4 + m // 3)
                            sp_.sem_inc(sp_tick, 1)
                        elif m == NRAW - 1:
                            sp_.wait_ge(m_lo_pool, (E + 1) * r)
                            sp_.sem_inc(sp_tick, 1)
                    if m < 2:
                        gate_up_unit(0, m, m, m)
                    elif (m + 1) % 3 == 2:
                        down_unit(i - 1, m, m)
                    else:
                        gate_up_unit(i, (m + 1) % 3, m, m)

                def few_in_flight(i, b, c):
                    u = 3 * b + c - AHEAD
                    group = i // BODY if isinstance(i, int) else (i - b) // BODY
                    sp_.wait_ge(m_ld[u % NRAW], 32 * (3 * E // NRAW * r + group + 1 + u // NRAW))
                    sp_.sem_inc(sp_tick, 1)

                def step(i, b):
                    m = 3 * i
                    few_in_flight(i, b, 0)
                    gate_up_unit(i, 1, m, 3 * b)
                    few_in_flight(i, b, 1)
                    sp_.wait_ge(m_lo_pool, (E + 1) * r + i - 3)
                    sp_.sem_inc(sp_tick, 1)
                    down_unit(i - 1, m + 1, 3 * b + 1)
                    few_in_flight(i, b, 2)
                    gate_up_unit(i + 1, 0, m + 2, 3 * b + 2)

                for m in range(NRAW):
                    first(m)
                with sp_.Fori(1, E // BODY - 1) as j:
                    for b in range(BODY):
                        step(BODY * j + b, b)
                for b in range(BODY - 1):
                    step(E - BODY + b, b)
                gate_up_unit(E - 1, 1, 3 * E - 3, NRAW - 3)
                sp_.wait_ge(m_lo_pool, (E + 1) * r + E - 4)
                sp_.sem_inc(sp_tick, 1)
                down_unit(E - 2, 3 * E - 2, NRAW - 2)
                down_unit(E - 1, 3 * E - 1, NRAW - 1)

            moe_loads(0)
            sp_.wait_ge(flag_ok, 1)
            more = sp_.value_load(flag[0:1, 0:1], min_val=0, max_val=1)
            with sp_.If(more != 0):
                with sp_.Fori(1, ROUNDS) as r:
                    moe_loads(r)
            for t in range(NT):
                sp_.wait_ge(y_ok, t + 1)
                dst = y_prompt[0, tok(t), :] if t < NT - 1 else y_sample[0, :, :]
                sp_.dma_start(dst, x_sb[0:rows[t], t, :]).then_inc(y_out, 16)
            sp_.wait_ge(y_out, 16 * NT)

        @block.gpsimd
        def _(pool):
            chain = [0]

            def link(ins):
                chain[0] += 1
                ins.then_inc(pch, 1)
                pool.wait_ge(pch, chain[0])

            link(pool.memset(ident[:, :], 0.0))
            link(pool.affine_select(out=ident[:, :], in_=ident[:, :], compare_op=ALU.not_equal, fill=1.0, base=0,
                                    pattern=[[-1, P]], channel_multiplier=1))
            pool.tensor_copy(identb[:, :], ident[:, :]).then_inc(pc, 1)
            pool.dma_start(ws, gm_w_s[0].rearrange("g t s -> t g s")).then_inc(ld_ws, 16)
            link(pool.memset(mhalf[:, :], -0.5))

            def inv_root(dst, s, width):
                link(pool.tensor_scalar(s, s, 1.0 / width, EPS, ALU.mult, ALU.add))
                n = s.shape[-1]
                return pool.tensor_tensor(dst, s, mhalf[0:s.shape[0], 0:n], ALU.pow)

            for t in range(NT):
                pool.wait_ge(ssq1_ok, t + 1)
                inv_root(rstd[0:rows[t], 0, t:t + 1], ssq[0:rows[t], 0, t:t + 1], D).then_inc(rstd1_ok, 1)
                if t == 1:
                    pool.wait_ge(ld_ws, 16)
                    pool.affine_select(out=ws, in_=ws, compare_op=ALU.is_ge, fill=0.0, base=0,
                                       pattern=[[0, GROUPS], [-1, P]], channel_multiplier=1).then_inc(ws_masked, 1)

            link(pool.memset(maskneg[:, :], 0.0))
            link(pool.affine_select(out=maskneg[:, :], in_=maskneg[:, :], compare_op=ALU.is_gt, fill=NEG, base=0,
                                    pattern=[[1, P]], channel_multiplier=-1))
            for h in range(HEADS):
                ins = pool.tensor_copy(maskneg8[:, h, :], maskneg[0:DEC, 0:DEC])
            ins.then_inc(pc, 1)
            link(pool.memset(negU[:, :], -1.0))
            pool.memset(negones[:, :], -1.0)
            pool.affine_select(out=negU[:, :], in_=negU[:, :], compare_op=ALU.is_ge, fill=0.0, base=0,
                               pattern=[[-1, P]], channel_multiplier=1).then_inc(pc, 1)
            link(pool.memset(before[:, :], 1.0))
            pool.memset(onesb[:, :], 1.0)
            pool.affine_select(out=before[:, :], in_=before[:, :], compare_op=ALU.is_gt, fill=0.0, base=0,
                               pattern=[[1, P]], channel_multiplier=-1).then_inc(pc, 1)
            pool.memset(qs[:, :], 0.0)
            pool.memset(qpad[:, :, :], 0.0).then_inc(pc, 1)
            link(pool.iota(iota_i[:, :], pattern=[[1, CAP]], base=0, channel_multiplier=0))
            link(pool.tensor_copy(iota_e[:, :], iota_i[:, 0:E]))
            pool.tensor_scalar(prio[:, :], iota_e[:, 0:EPG], -1.0, float(EPG), ALU.mult, ALU.add)
            link(pool.tensor_copy(slot_no[:, :], iota_i[:, :]))
            pool.iota(iota_i[:, 0:NT], pattern=[[0, NT]], base=0, channel_multiplier=1)
            link(pool.iota(iota_i[:, NT:2 * NT], pattern=[[P, NT]], base=0, channel_multiplier=0))
            link(pool.tensor_copy(tok_part[:, :, :], iota_i[:, 0:2 * NT].rearrange("p (a t) -> p a t", a=2)))
            for a in range(2):
                pool.affine_select(out=tok_part[:, a, :], in_=tok_part[:, a, :], compare_op=ALU.is_ge, fill=0.0, base=TOK - 1,
                                   pattern=[[-P, NT]], channel_multiplier=-1)
            link(pool.memset(valid[:, :], 1.0))
            pool.affine_select(out=valid[:, :], in_=valid[:, :], compare_op=ALU.is_ge, fill=0.0, base=TOK - 1,
                               pattern=[[-P, NT]], channel_multiplier=-1).then_inc(pc, 1)

            for t in range(NT):
                pool.wait_ge(gv_ssq, t + 1)
                inv_root(rstd[0:rows[t], 1, t:t + 1], ssq[0:rows[t], 1, t:t + 1], CB).then_inc(gv_rstd, 1)
            pool.wait_ge(gvn_ok, NT)
            pool.dma_start(gv_sample[0, 0].rearrange("t g d -> t (g d)"), gvn[0:DEC, NT - 1, :]).then_inc(st_out, 16)

            for b in range(2):
                pool.wait_ge(ld_kg if b else ld_qg, 16)
                if b == 0:
                    link(pool.tensor_scalar(qg[:, :], qg[:, :], HD ** -0.5, 0.0, ALU.mult, ALU.add))
                for t in range(NT):
                    m, p = NT * b + t, rows[t]
                    pool.wait_ge(ssq8_ok, m + 1)
                    inv_root(rstd8[0:p, m, :], ssq8[0:p, m, :], HD).then_inc(rstd8_ok, 1)
                    pool.wait_ge(qk_scaled, m + 1)
                    q3 = qn[m % 2][0:p, :].rearrange("p (h d) -> p h d", h=HEADS)
                    g = (kg if b else qg)[0:p, :].rearrange("p (a d) -> p a d", a=1).broadcast_to([p, HEADS, HD])
                    pool.tensor_tensor(q3, q3, g, ALU.mult).then_inc(qk_ok, 1)

            pool.wait_ge(w_ok, 2 * NH)
            pool.wait_ge(pv_ok, NV)
            pool.wait_ge(ld_wr, 16 * (NG + 1))
            link(pool.memset(wr_pad[:, :, :], 0.0))
            pool.tensor_copy(wr_pad[:, :, 0:NE], wr[:, :, :]).then_inc(wr_padded, 1)
            pool.dma_start(g2b[:, :], norm2_g.broadcast_to([P, D])).then_inc(ld_g2, 16)
            for t in range(NT):
                pool.wait_ge(ssq2_ok, 2 * t + 2)
                link(pool.tensor_tensor(ssq[0:rows[t], 2, t:t + 1], ssq[0:rows[t], 2, t:t + 1], ssq[0:rows[t], 3, t:t + 1], ALU.add))
                inv_root(rstd[0:rows[t], 2, t:t + 1], ssq[0:rows[t], 2, t:t + 1], D).then_inc(rstd2_ok, 1)
                if t < 4:
                    c = slice(t * UNIT // 4, (t + 1) * UNIT // 4)
                    pool.wait_ge(m_hi, 1)
                    ins = pool.tensor_tensor(wlo[SPLIT_OF[0]][:, c], eraw[0][:, c], whi[SPLIT_OF[0]][:, c].bitcast(F32), ALU.subtract)
                    if t == 3:
                        ins.then_inc(m_lo, 1)

            def moe_gathers(r):
                s0, u0 = E * r, 3 * E * r
                for m in range(1 if isinstance(r, int) else 0, 3):
                    pool.wait_ge(m_hi, u0 + m + 1)
                    pool.sem_inc(pool_tick, 1)
                    pool.tensor_tensor(wlo[SPLIT_OF[m]][:, :], eraw[m][:, :], whi[SPLIT_OF[m]][:, :].bitcast(F32), ALU.subtract)\
                        .then_inc(m_lo, 1)
                pool.sem_inc(m_lo_pool, 1)
                if isinstance(r, int):
                    for i in range(3):
                        pool.wait_ge(xn_st[i], 16 * len(xn2_tiles[i]))
                pool.wait_ge(idx_ok, r + 1)
                pool.sem_inc(pool_tick, 1)

                def gather(i, p):
                    s = s0 + i
                    if not (isinstance(s, int) and s < 2):
                        pool.wait_ge(xs_tr, 2 * (s - 1))
                        pool.sem_inc(pool_tick, 1)
                    pool.tensor_copy(idx_cur[p][:, :], idx_all[:, bass.ds(i, 1)]).then_inc(idx_cp, 1)
                    pool.wait_ge(idx_cp, s + 1)
                    pool.sem_inc(pool_tick, 1)
                    pool.indirect_dma_start(xs[p][:, :], None, xn_dram[:, :],
                                            bass.IndirectOffsetOnAxis(ap=idx_cur[p][:, 0:1], axis=0)).then_inc(xs_ld[p], 16)

                def lo(i, j, a):
                    m = 3 * i + 1 if not (isinstance(i, int) and i == E) else 3 * E - 1
                    slot = unit_at(i, 2, j, a)[0] if not (isinstance(i, int) and i == E) else (3 * E - 1) % NRAW
                    split = SPLIT_OF[1] if not (isinstance(i, int) and i == E) else SPLIT_OF[2]
                    pool.wait_ge(m_hi, u0 + m + 1)
                    pool.sem_inc(pool_tick, 1)
                    pool.tensor_tensor(wlo[split][:, D:2 * D], eraw[slot][:, D:2 * D], whi[split][:, D:2 * D].bitcast(F32),
                                       ALU.subtract).then_inc(m_lo_pool, 1)

                def store(i, p):
                    s = s0 + i
                    pool.wait_ge(y_act, s + 1)
                    pool.wait_ge(y_dve, s + 1)
                    pool.dma_start(y_dram[bass.ds(r * SLOTS + i * CAP, CAP), :], yout[p][:, :]).then_inc(y_st[p], 16)

                def step(i, j, a, p):
                    if not (isinstance(i, int) and i >= E - 2):
                        gather(i + 2, p)
                    if not (isinstance(i, int) and i == 0):
                        lo(i, j, a)
                    if not (isinstance(i, int) and i < 2):
                        store(i - 2, p)

                gather(0, 0)
                gather(1, 1)
                for i in range(3):
                    step(i, 0, 0, i % 2)
                with pool.Fori(0, (E - 4) // BODY - 1) as j:
                    for a in range(BODY):
                        step(BODY * j + 3 + a, j, a, (3 + a) % 2)
                for i in range(E - 1 - BODY, E):
                    step(i, 0, 0, i % 2)
                lo(E, 0, 0)
                store(E - 2, 0)
                store(E - 1, 1)
                for p in range(2):
                    pool.wait_ge(y_st[p], 16 * (E // 2) * (r + 1))

            def fetch(n):
                pool.wait_ge(places_ok, 1)
                for t in range(NT):
                    for c in range(2):
                        pool.indirect_dma_start(yg[c][t][0:rows[t], :], None, y_dram[0:n, :],
                                                bass.IndirectOffsetOnAxis(ap=pos_y[c][0:rows[t], t:t + 1], axis=0))\
                            .then_inc(yg_ld[t], 16)

            moe_gathers(0)
            pool.wait_ge(flag_ok, 1)
            more = pool.value_load(flag[0:1, 0:1], min_val=0, max_val=1)
            with pool.If(more != 0):
                with pool.Fori(1, ROUNDS) as r:
                    moe_gathers(r)
                fetch(ROUNDS * SLOTS)
            with pool.Else():
                fetch(SLOTS)
            pool.wait_ge(st_out, 16)
            pool.wait_ge(v_out, 16 * NT)
            for i in range(2):
                pool.wait_ge(k_out[i], K_STORED[i])

        @block.scalar
        def _(act):
            act.dma_start(g1b[:, :], norm1_g.broadcast_to([P, D])).then_inc(ld_g1, 16)
            act.preload_act_table_set("gelu_apprx_tanh_and_others")

            def split_hi(n):
                act.wait_ge(ld_raw[n % 3], 16 * (n // 3 + 1))
                if n >= 2:
                    unit_used(act, n - 2)
                act.activation(whi[n % 2][:, :], raw[n % 3][:, :], ACT.Copy).then_inc(hi_ok, 1)

            def square_x(t):
                act.wait_ge(ld_x[t], 16)
                if t >= 1:
                    act.wait_ge(ssq1_ok, t)
                act.activation(v_sb[0:rows[t], 0:2, :].rearrange("p a n -> p (a n)"), x_sb[0:rows[t], t, :], ACT.Square,
                               accum_out=ssq[0:rows[t], 0, t:t + 1]).then_inc(ssq1_ok, 1)

            def x_hi(t):
                for b in range(2):
                    act.wait_ge(x_tr, 2 * t + b + 1)
                    src = turn_bank(X_USE + 2 * t + b)[:, :].rearrange("p (k n) -> p k n", k=4)
                    act.activation(xT_hi[:, 4 * b:4 * b + 4, tok(t)], src, ACT.Copy).then_inc(xT_hi_ok, 1)

            square_x(0)
            square_x(1)
            x_hi(0)
            split_hi(0)
            x_hi(1)
            square_x(2)
            square_x(3)
            split_hi(1)
            square_x(4)
            x_hi(2)
            x_hi(3)
            act.dma_start(gvb[:, :], gm_v_norm_g.broadcast_to([P, CB])).then_inc(ld_gvb, 16)
            act.dma_start(qg[:, :], q_norm_g.broadcast_to([P, HD])).then_inc(ld_qg, 16)
            act.dma_start(kg[:, :], k_norm_g.broadcast_to([P, HD])).then_inc(ld_kg, 16)
            act.dma_start(bs_col[:, :], gm_b_s[0].rearrange("g t -> t g"), allow_slow_non_contiguous=True).then_inc(ld_bs, 16)
            act.dma_start(wr[:, :, 0:NG], w_rg[0].rearrange("(k p) g -> p k g", p=P)).then_inc(ld_wr, 16)
            for g in range(NG):
                act.dma_start(wr[:, :, NG + g * EPG:NG + (g + 1) * EPG], w_re[0, g].rearrange("(k p) e -> p k e", p=P))\
                   .then_inc(ld_wr, 16)
            act.dma_start(br[:, 0:NG], b_rg.broadcast_to([P, NG])).then_inc(ld_br, 16)
            act.dma_start(br[:, NG:NE], b_re.rearrange("l g e -> l (g e)").broadcast_to([P, E])).then_inc(ld_br, 16)
            act.wait_ge(ws_tr, 1)
            act.activation(WmT[:, :, :].rearrange("p g s -> p (g s)"), bank[7][:, :], ACT.Copy).then_inc(wmT_ok, 1)
            act.wait_ge(x_tr, 2 * NT)
            for c2 in range(2):
                act.dma_start(xn[c2][:, :].rearrange("p (c n) -> p c n", c=2),
                              cache_k[0, 0, 2 * c2 * P:2 * (c2 + 1) * P].rearrange("(c p) h d -> p c (h d)", p=P))\
                   .then_inc(ld_ck[c2], 16)
            act.dma_start(cv[:, :, :], cache_v[0, 0].rearrange("(c p) h d -> p c (h d)", p=P)).then_inc(ld_cv, 16)

            def exp_log(h):
                b_ = lw[h % 5]
                pieces = [[b_[:, 0:512]], [b_[:, 512:ZW]] if h else [b_[:, 512:1024], b_[0:DEC, 1024:ZW]]]
                for a in range(2):
                    act.wait_ge(az_ok, 2 * h + a + 1)
                    for x in pieces[a]:
                        ins = act.activation(x, x, ACT.Exp, scale=-1.0)
                    ins.then_inc(e_ok, 1)
                for a in range(2):
                    act.wait_ge(e_ok, 2 * h + a + 1)
                    for x in pieces[a]:
                        ins = act.activation(x, x, ACT.Ln, bias=1.0)
                    ins.then_inc(l_ok, 1)

            for b, name in enumerate(BLOCKS):
                if name in ("k", "v"):
                    for t in range(NT):
                        m = NT * (name == "v") + t
                        act.wait_ge(qk_tr, m + 1)
                        src = turn_bank(QK_USE + m)[:, :].rearrange("p (j n) -> p j n", j=KCH)[:, :, 0:rows[t]]
                        if name == "v":
                            act.activation(kT[:, :, tok(t)], src, ACT.Copy).then_inc(qkT_ok, 1)
                            dst = k_prompt[0, 0, tok(t)] if t < NT - 1 else k_sample[0, 0]
                            act.dma_start(dst.rearrange("t h d -> t (h d)"), qn[m % 2][0:rows[t], :]).then_inc(k_out[m % 2], 16)
                        else:
                            if t == 0:
                                act.wait_ge(pc, PC_QPAD)
                            if t < NT - 1:
                                q4 = qpad[:, :, :].rearrange("p (j a) n -> p j a n", a=2)
                                act.activation(q4[0:HD, :, 0, tok(t)], src[0:HD], ACT.Copy)
                                act.activation(q4[HD:P, :, 1, tok(t)], src[HD:P], ACT.Copy).then_inc(qkT_ok, 1)
                            else:
                                for odd in range(2):
                                    act.activation(pairs(qs[0:HD, :], odd, 0), src[0:HD, odd:KCH:2], ACT.Copy)
                                    ins = act.activation(pairs(qs[HD:P, :], odd, 1), src[HD:P, odd:KCH:2], ACT.Copy)
                                ins.then_inc(qkT_ok, 1)
                split_hi(2 * b + 2)
                if name == "v":
                    act.preload_act_table_set("natural_log_exp_and_others")
                    exp_log(0)
                for t in range(NT):
                    p = rows[t]
                    act.wait_ge(proj_done, NT * b + t + 1)

                    def evict(dst, func):
                        for a, c in block_parts(t):
                            ins = act.activation(dst[0:p, c], a, func)
                        return ins

                    if name == "gv":
                        evict(gvn[:, t, :], ACT.Gelu_apprx_tanh).then_inc(gv_gelu, 1)
                    elif name == "u":
                        if t >= 2:
                            act.wait_ge(gm_ok, t - 1)
                        evict(ut[t % 2], ACT.Gelu_apprx_tanh).then_inc(acc_free[t], 1)
                    elif name in ("q", "k"):
                        m = NT * (b - 2) + t
                        if m >= 2:
                            act.wait_ge(ssq8_ok, m - 1)
                        evict(sqt[m % 2], ACT.Square).then_inc(sq_ok, 1)
                    else:
                        evict(v_sb[:, t, :], ACT.Copy).then_inc(v_ok, 1)
                        dst = v_prompt[0, 0, tok(t)] if t < NT - 1 else v_sample[0, 0]
                        act.wait_ge(v_ok, t + 1)
                        act.dma_start(dst.rearrange("t h d -> t (h d)"), v_sb[0:p, t, :]).then_inc(v_out, 16)
                if b == 0:
                    for c in range(NCH):
                        act.wait_ge(ck_tr, c + 1)
                        act.activation(ckT[:, :, c * P:(c + 1) * P],
                                       turn_bank(CK_USE + c)[:, :].rearrange("p (j n) -> p j n", j=KCH), ACT.Copy)\
                           .then_inc(ckT_ok, 1)
                if name != "v":
                    split_hi(2 * b + 3)

            def weights(h):
                act.wait_ge(sp_ok, h + 1)
                for a in range(2):
                    act.wait_ge(rest_ok, 2 * h + a + 1)
                    for bk, p, c in parts_of(h, a):
                        ins = act.activation(lw[h % 5][0:p, c], z_of(h)[bk][0:p, 0:c.stop - c.start], ACT.Exp)
                    ins.then_inc(w_ok, 1)

            def sb_hi(v):
                act.wait_ge(pv_ok, v + 1)
                act.activation(xT_hi[:, KCH + v - 1, :], bank[5 + v % 2][:, :], ACT.Copy).then_inc(sbT_hi, 1)

            for t in range(NT - 1):
                act.wait_ge(gm_tr, t + 1)
                src = bank[3 + t % 2][:, :].rearrange("p (k n) -> p k n", k=KCH)
                act.activation(xT_hi[:, 0:KCH, tok(t)], src, ACT.Copy).then_inc(gmT_hi, 1)
            for h in range(NH):
                if h + 1 < NH:
                    exp_log(h + 1)
                weights(h)
                if h == 7:
                    split_hi(U_IN + 1)
                if h >= 5 and h % 2:
                    sb_hi(h // 2 - 1)
            sb_hi(NV - 2)
            sb_hi(NV - 1)

            def first_hi(m):
                act.wait_ge(m_ld[m], 32)
                act.activation(whi[SPLIT_OF[m]][:, :], eraw[m][:, :], ACT.Copy).then_inc(m_hi, 1)

            split_hi(U_IN + 2)
            split_hi(U_IN + 3)
            unit_used(act, U_IN + 2)
            first_hi(0)
            first_hi(1)

            def square_h(t):
                act.wait_ge(acc_free[t], 3)
                for n in range(2):
                    act.activation(bank[t][0:rows[t], :], x_sb[0:rows[t], t, n * CB:(n + 1) * CB], ACT.Square,
                                   accum_out=ssq[0:rows[t], 2 + n, t:t + 1]).then_inc(ssq2_ok, 1)
                    act.wait_ge(ssq2_ok, 2 * t + n + 1)

            def x2T_copy(t):
                if t == NT - 2:
                    unit_used(act, U_IN + 3)
                elif t >= 1:
                    act.wait_ge(r_mm, t if t < NT - 1 else t - 1)
                for b in range(2):
                    act.wait_ge(x2_tr, 2 * t + b + 1)
                    src = bank[5 + b][:, :].rearrange("p (k n) -> p k n", k=4)[:, :, 0:rows[t]]
                    act.activation(x2T_of[t][:, 4 * b:4 * b + 4, 0:rows[t]], src, ACT.Copy).then_inc(x2T_ok, 1)

            def store_normed(t):
                act.wait_ge(xn2_ok, t + 1)
                act.dma_start(xn_dram[tok(t), :], xn2_of[t][0:rows[t]]).then_inc(xn_st[2 if t == NT - 1 else t % 2], 16)

            square_h(0)
            square_h(1)
            for t in range(2, NT):
                store_normed(t - 2)
                square_h(t)
                x2T_copy(t - 2)
            store_normed(NT - 2)
            x2T_copy(NT - 2)
            store_normed(NT - 1)
            x2T_copy(NT - 1)
            unit_used(act, U_IN + 3)
            first_hi(2)
            act.wait_ge(rx, 1)
            act.activation(r4[1][:, :, :], r4[0][:, :, :], ACT.Exp).then_inc(r_exp, 1)
            act.wait_ge(rx, 2)
            act.activation(r1[5][:, :], r1[4][:, :], ACT.Exp).then_inc(r_exp, 1)
            act.preload_act_table_set("silu_and_others")

            def moe(r):
                s0, u0 = E * r, 3 * E * r

                def hi(m3, at, unit):
                    slot, group = at
                    act.wait_ge(m_ld[slot], 32 * (3 * E // NRAW * r + group + 1))
                    if not (isinstance(unit, int) and unit < 3):
                        act.wait_ge(m_used, unit - 2)
                    act.activation(whi[SPLIT_OF[m3]][:, :], eraw[slot][:, :], ACT.Copy).then_inc(m_hi, 1)

                def tokens_hi(i, p):
                    s = s0 + i
                    for b in range(2):
                        act.wait_ge(xs_tr, 2 * s + b + 1)
                        if b == 0 and not (isinstance(i, int) and i < 2):
                            act.wait_ge(m_used, u0 + gate_up_used(i - 2))
                        act.activation(xsT_hi[p][:, 4 * b:4 * b + 4, :].rearrange("p k n -> p (k n)"),
                                       bank[5 + b][:, 0:4 * CAP], ACT.Copy).then_inc(xsT_hi_ok, 1)

                def silu(i, p):
                    s = s0 + i
                    act.wait_ge(m_used, u0 + gate_up_used(i))
                    if not (isinstance(s, int) and s < 2):
                        act.wait_ge(a_tr, s - 1)
                    act.activation(sg[p][:, :], bank[p][0:CAP, 0:FF], ACT.Silu).then_inc(silu_ok, 1)

                def act_hi(i, p):
                    s = s0 + i
                    act.wait_ge(a_tr, s + 1)
                    if not (isinstance(i, int) and i < 2):
                        act.wait_ge(m_used, u0 + down_used(i - 2))
                    act.activation(aT_hi[p][:, :, :].rearrange("p k n -> p (k n)"), bank[7][:, 0:2 * CAP], ACT.Copy)\
                       .then_inc(aT_hi_ok, 1)

                def out_rows(i, p, n):
                    act.wait_ge(m_used, u0 + down_used(i))
                    if not (isinstance(r, int) and isinstance(i, int) and i < 2):
                        act.wait_ge(y_st[p], 16 * ((E // 2) * r + n))
                    act.activation(yout[p][:, 0:CB], bank[2][0:CAP, :], ACT.Copy).then_inc(y_act, 1)

                def step(i, j, a):
                    first = isinstance(i, int) and i == 0
                    last = isinstance(i, int) and i == E - 1
                    p = i % 2 if isinstance(i, int) else (3 + a) % 2
                    if not first:
                        hi(1, unit_at(i, 2, j, a), u0 + 3 * i + 1)
                        act_hi(i - 1, 1 - p)
                    if not first:
                        hi(2, unit_at(i, 3, j, a), u0 + 3 * i + 2)
                    if first:
                        hi(0, unit_at(i, 4, j, a), u0 + 3)
                    if not last:
                        tokens_hi(i + 1, 1 - p)
                    silu(i, p)
                    if not first and not last:
                        hi(0, unit_at(i, 4, j, a), u0 + 3 * i + 3)
                    if not first:
                        out_rows(i - 1, 1 - p, half_of(i - 1, j, 2 + a))

                if not isinstance(r, int):
                    for m in range(3):
                        hi(m, (m, 0), u0 + m)
                tokens_hi(0, 0)
                for i in range(3):
                    step(i, 0, 0)
                with act.Fori(0, (E - 4) // BODY) as j:
                    for a in range(BODY):
                        step(BODY * j + 3 + a, j, a)
                step(E - 1, 0, 0)
                act_hi(E - 1, 1)
                out_rows(E - 1, 1, E // 2 - 1)

            moe(0)
            act.wait_ge(flag_ok, 1)
            more = act.value_load(flag[0:1, 0:1], min_val=0, max_val=1)
            with act.If(more != 0):
                with act.Fori(1, ROUNDS) as r:
                    moe(r)

        @block.vector
        def _(dve):
            chain = [0]

            def link(ins):
                chain[0] += 1
                ins.then_inc(dch, 1)
                dve.wait_ge(dch, chain[0])

            def split_lo(n):
                dve.wait_ge(hi_ok, n + 1)
                dve.tensor_tensor(wlo[n % 2][:, :], raw[n % 3][:, :], whi[n % 2][:, :].bitcast(F32), ALU.subtract)\
                   .then_inc(lo_ok, 1)

            def square_sum(dst, x, junk):
                return dve.tensor_tensor_reduce(junk, x, x, 1.0, 0.0, ALU.mult, ALU.add, dst)

            def norm_x(t):
                p = rows[t]
                dve.wait_ge(rstd1_ok, t + 1)
                if t == 0:
                    dve.wait_ge(ld_g1, 16)
                if t >= 2:
                    dve.wait_ge(x_tr, 2 * (t - 1))
                dve.scalar_tensor_tensor(out=xn[t % 2][0:p, :], in0=x_sb[0:p, t, :], scalar=rstd[0:p, 0, t:t + 1],
                                         in1=g1b[0:p, :], op0=ALU.mult, op1=ALU.mult).then_inc(xn_ok, 1)

            def x_lo(t):
                for b in range(2):
                    src = turn_bank(X_USE + 2 * t + b)[:, :].rearrange("p (k n) -> p k n", k=4)[:, :, 0:rows[t]]
                    if t == NT - 1:
                        dve.wait_ge(x_tr, 2 * t + b + 1)
                        dve.tensor_copy(xT_s[:, 4 * b:4 * b + 4, :], src).then_inc(xT_lo_ok, 1)
                        continue
                    dve.wait_ge(xT_hi_ok, 2 * t + b + 1)
                    dve.tensor_tensor(xT_lo[:, 4 * b:4 * b + 4, tok(t)], src,
                                      xT_hi[:, 4 * b:4 * b + 4, tok(t)].bitcast(F32), ALU.subtract).then_inc(xT_lo_ok, 1)

            norm_x(0)
            norm_x(1)
            x_lo(0)
            split_lo(0)
            norm_x(2)
            x_lo(1)
            norm_x(3)
            x_lo(2)
            norm_x(4)
            x_lo(3)
            split_lo(1)
            x_lo(4)

            def abs_z(h):
                if h >= 4:
                    dve.wait_ge(pv_ok, (h - 4) // 2 + 1)
                for a in range(2):
                    dve.wait_ge(z_ok, 2 * h + a + 1)
                    for bk, p, c in parts_of(h, a):
                        ins = dve.tensor_scalar(lw[h % 5][0:p, c].bitcast(I32), z_of(h)[bk][0:p, 0:c.stop - c.start].bitcast(I32),
                                                0x7FFFFFFF, None, ALU.bitwise_and)
                    ins.then_inc(az_ok, 1)

            def softplus(h):
                if h >= 2:
                    dve.wait_ge(rest_ok, 2 * (h - 1))
                s, u = sp[h % 2], later_sums(h)
                if h == 0:
                    link(dve.memset(s[:, 1024:ZW], 0.0))
                for a in range(2):
                    dve.wait_ge(l_ok, 2 * h + a + 1)
                    for bk, p, c in parts_of(h, a):
                        ins = dve.scalar_tensor_tensor(out=s[0:p, c], in0=z_of(h)[bk][0:p, 0:c.stop - c.start], scalar=0.0,
                                                       in1=lw[h % 5][0:p, c], op0=ALU.max, op1=ALU.add)
                ins.then_inc(sp_ok, 1)
                dve.wait_ge(sp_ok, h + 1)
                n = P if h else DW
                if h == 1:
                    dve.wait_ge(rest_ok, 2)
                if h:
                    adds = ((2, s[:, 1152:1280], s[:, 896:1024]), (1, s[:, 768:896], u[:, 2 * P:3 * P]),
                            (0, s[:, 640:768], s[:, 1024:1152]))
                else:
                    adds = ((2, s[:, 768:1024], s[:, 1024:1280]), (1, s[:, 512:768], u[:, 2 * n:3 * n]),
                            (0, s[:, 256:512], u[:, n:2 * n]))
                for k, a, b in adds:
                    ins = dve.tensor_tensor(u[:, k * n:(k + 1) * n], a, b, ALU.add)
                    if k:
                        link(ins)
                ins.then_inc(later_ok, 1)

            for b, name in enumerate(BLOCKS):
                split_lo(2 * b + 2)
                for t in range(NT):
                    p = rows[t]
                    if name == "gv":
                        dve.wait_ge(gv_gelu, t + 1)
                        square_sum(ssq[0:p, 1, t:t + 1], gvn[0:p, t, :], sqt[0][0:p, :]).then_inc(gv_ssq, 1)
                        if t == 0:
                            dve.wait_ge(ld_gvb, 16)
                        dve.wait_ge(gv_rstd, t + 1)
                        dve.scalar_tensor_tensor(out=gvn[0:p, t, :], in0=gvn[0:p, t, :], scalar=rstd[0:p, 1, t:t + 1],
                                                 in1=gvb[0:p, :], op0=ALU.mult, op1=ALU.mult).then_inc(gvn_ok, 1)
                    elif name == "u":
                        dve.wait_ge(acc_free[t], 1)
                        dve.wait_ge(mixed, t + 1)
                        if t == 0:
                            dve.wait_ge(ld_bs, 16)
                        if t == NT - 1:
                            dve.wait_ge(st_out, 16)
                        for g in range(GROUPS):
                            c = slice(g * P, (g + 1) * P)
                            ins = dve.scalar_tensor_tensor(out=gvn[0:p, t, c], in0=bank[7][0:p, c], scalar=bs_col[0:p, g:g + 1],
                                                           in1=ut[t % 2][0:p, c], op0=ALU.add, op1=ALU.mult)
                        ins.then_inc(gm_ok, 1)
                    elif name in ("q", "k"):
                        m = NT * (b - 2) + t
                        dve.wait_ge(sq_ok, m + 1)
                        dve.tensor_reduce(ssq8[0:p, m, :], sqt[m % 2][0:p, :].rearrange("p (h d) -> p h d", h=HEADS), AX.X,
                                          ALU.add).then_inc(ssq8_ok, 1)
                        dve.wait_ge(rstd8_ok, m + 1)
                        if m >= 2:
                            dve.wait_ge(qk_tr, m - 1)
                        if m >= NT + 2:
                            dve.wait_ge(k_out[m % 2], 16 * sum(x % 2 == m % 2 for x in range(NT, m)))
                        for a, c in block_parts(t):
                            n = (c.stop - c.start) // HD
                            rb = rstd8[0:p, m, c.start // HD:c.stop // HD].rearrange("p (h a) -> p h a", a=1).broadcast_to([p, n, HD])
                            ins = dve.tensor_tensor(qn[m % 2][0:p, c].rearrange("p (h d) -> p h d", h=n),
                                                    a.rearrange("p (h d) -> p h d", h=n), rb, ALU.mult)
                        ins.then_inc(qk_scaled, 1)
                if name == "v":
                    for i in range(2):
                        dve.wait_ge(k_out[i], K_STORED[i])
                    abs_z(0)
                    softplus(0)
                if name != "v":
                    split_lo(2 * b + 3)

            def sb_lo(v):
                o = bank[5 + v % 2]
                if v:
                    dve.wait_ge(sbT_hi, v)
                    dve.tensor_tensor(xT_lo[:, KCH + v - 1, :], o[:, :], xT_hi[:, KCH + v - 1, :].bitcast(F32), ALU.subtract)\
                       .then_inc(sbT_lo, 1)
                else:
                    dve.wait_ge(pv_ok, 1)
                    for odd in range(2):
                        for a in range(2):
                            r = slice(HD * a, HD * (a + 1))
                            ins = dve.tensor_copy(xT_s[r, KCH + odd:KC:2, :], pairs(o[r, :], odd, a))
                    ins.then_inc(sbT_lo, 1)

            for t in range(NT):
                src = bank[3 + t % 2][:, :].rearrange("p (k n) -> p k n", k=KCH)[:, :, 0:rows[t]]
                if t == NT - 1:
                    dve.wait_ge(gm_tr, t + 1)
                    dve.tensor_copy(xT_s[:, 0:KCH, :], src).then_inc(gmT_lo, 1)
                    continue
                dve.wait_ge(gmT_hi, t + 1)
                dve.tensor_tensor(xT_lo[:, 0:KCH, tok(t)], src, xT_hi[:, 0:KCH, tok(t)].bitcast(F32), ALU.subtract)\
                   .then_inc(gmT_lo, 1)
            for h in range(NH):
                if h + 1 < NH:
                    abs_z(h + 1)
                    softplus(h + 1)
                if h == 1:
                    sb_lo(0)
                if h == 7:
                    split_lo(U_IN + 1)
                if h >= 5 and h % 2:
                    sb_lo(h // 2 - 1)
            sb_lo(NV - 2)
            sb_lo(NV - 1)

            split_lo(U_IN + 2)
            for t in range(NT):
                p = rows[t]
                dve.wait_ge(proj_done, NT * NB + t + 1)
                for a, c in block_parts(t):
                    ins = dve.tensor_tensor(x_sb[0:p, t, c], x_sb[0:p, t, c], a, ALU.add)
                ins.then_inc(acc_free[t], 1)
            split_lo(U_IN + 3)
            link(dve.memset(lg[:, :, :], 0.0))

            def norm_h(t):
                p = rows[t]
                dve.wait_ge(rstd2_ok, t + 1)
                if t == 0:
                    dve.wait_ge(ld_g2, 16)
                if 2 <= t < NT - 1:
                    dve.wait_ge(x2_tr, 2 * (t - 1))
                    dve.wait_ge(xn_st[t % 2], 16 * (t // 2))
                dve.scalar_tensor_tensor(out=xn2_of[t][0:p], in0=x_sb[0:p, t, :], scalar=rstd[0:p, 2, t:t + 1],
                                         in1=g2b[0:p, :], op0=ALU.mult, op1=ALU.mult).then_inc(xn2_ok, 1)

            def logits(t):
                dve.wait_ge(r_mm, t + 1)
                if t == 0:
                    dve.wait_ge(ld_br, 32)
                dve.tensor_tensor(lg[0:rows[t], t, :], bank[7][0:rows[t], 0:NE], br[0:rows[t], :], ALU.add).then_inc(lg_ok, 1)

            def add_last(t):
                dve.wait_ge(proj_done, NT * (NB + 1) + t + 1)
                for a, c in block_parts(t):
                    cd = slice(CB + c.start, CB + c.stop)
                    ins = dve.tensor_tensor(x_sb[0:rows[t], t, cd], x_sb[0:rows[t], t, cd], a, ALU.add)
                ins.then_inc(acc_free[t], 1)

            add_last(0)
            for t in range(1, NT):
                add_last(t)
                norm_h(t - 1)
                if t >= 3:
                    logits(t - 3)
            norm_h(NT - 1)
            for t in range(NT - 3, NT):
                logits(t)

            dve.wait_ge(lg_ok, NT)
            dve.wait_ge(pc, PC_R)
            G4, E4 = lg[:, :, 0:NG], lg[:, :, NG:NE].rearrange("p t (g e) -> p t g e", g=NG)

            def wide(a, n):
                return a[:, :].rearrange("p (t a) -> p t a", a=1).broadcast_to([P, NT, n])

            prio_b = prio[:, :].rearrange("p (a e) -> p a e", a=1).broadcast_to([P, NT, EPG])

            def first_max(dst, values, top, tmp, tmp1):
                link(dve.tensor_reduce(top[:, :], values, AX.X, ALU.max))
                link(dve.tensor_tensor(tmp[:, :, :], values, wide(top, EPG), ALU.is_equal))
                link(dve.tensor_tensor(tmp[:, :, :], tmp[:, :, :], prio_b, ALU.mult))
                link(dve.tensor_reduce(tmp1[:, :], tmp[:, :, :], AX.X, ALU.max))
                link(dve.tensor_tensor(dst[:, :, :], tmp[:, :, :], wide(tmp1, EPG), ALU.is_equal))

            goh, eoh = r4[2], (r4[3], r4[4])
            first_max(goh, G4, r1[0], r4[5], r1[1])
            dve.tensor_tensor(r4[0][:, :, :], G4, wide(r1[0], NG), ALU.subtract).then_inc(rx, 1)
            gb = goh[:, :, :].rearrange("p t (g a) -> p t g a", a=1).broadcast_to([P, NT, NG, EPG])
            link(dve.tensor_tensor(r16[:, :, :, :], E4, gb, ALU.mult))
            le = r4[5]
            link(dve.tensor_reduce(le[:, :, :], r16[:, :, :, :].rearrange("p t g e -> p t e g"), AX.X, ALU.add))
            link(dve.tensor_copy(r16[:, :, 0, :], le[:, :, :]))
            le1 = r16[:, :, 0, :]
            first_max(eoh[0], le1, r1[2], le, r1[1])
            link(dve.scalar_tensor_tensor(out=r16[:, :, 1, :], in0=eoh[0][:, :, :], scalar=NEG, in1=le1, op0=ALU.mult, op1=ALU.add))
            first_max(eoh[1], r16[:, :, 1, :], r1[3], le, r1[1])
            dve.tensor_tensor(r1[4][:, :], r1[3][:, :], r1[2][:, :], ALU.subtract).then_inc(rx, 1)
            for c in range(2):
                eb = eoh[c][:, :, :].rearrange("p t (a e) -> p t a e", a=1).broadcast_to([P, NT, NG, EPG])
                link(dve.tensor_tensor(sel[c][:, :, :, :], gb, eb, ALU.mult))
            s2 = [s[:, :, :, :].rearrange("p t g e -> p t (g e)") for s in sel]
            s16 = r16[:, :, :, :].rearrange("p t g e -> p t (g e)")
            link(dve.tensor_tensor(s16, s2[0], s2[1], ALU.add))
            dve.tensor_tensor(selb[:, :, :], s16, wide(valid, E), ALU.mult).then_inc(selb_ok, 1)
            for c in range(2):
                for a in range(2):
                    part = tok_part[:, a, :].rearrange("p (t a) -> p t a", a=1).broadcast_to([P, NT, E])
                    dve.tensor_tensor(ids_of[:, c * NT:(c + 1) * NT, a * E:(a + 1) * E], s2[c], part, ALU.mult)
            dve.wait_ge(rank_ok, 1)
            rank = bank[7][:, 0:NT * E].rearrange("p (t e) -> p t e", e=E)
            dve.tensor_tensor(rk16[0][:, :, :], rank, s2[0], ALU.mult)
            link(dve.tensor_tensor(rk16[1][:, :, :], rank, s2[1], ALU.mult))
            dve.tensor_reduce(rank_of[0][:, :], rk16[0][:, :, :], AX.X, ALU.add)
            link(dve.tensor_reduce(rank_of[1][:, :], rk16[1][:, :, :], AX.X, ALU.add))

            def token_slots():
                slots = slot_no[:, :].rearrange("p (a s) -> p a s", a=1).broadcast_to([P, NT, CAP])
                for c in range(2):
                    ins = dve.tensor_tensor(onehot[:, c * NT:(c + 1) * NT, :], slots, wide(rank_of[c], CAP), ALU.is_equal)
                ins.then_inc(onehot_ok, 1)

            def slot_tokens(r):
                dve.wait_ge(ids_mm, r + 1)
                dve.tensor_copy(idx_rows[:, :], bank[4][0:CAP, 0:E]).then_inc(idx_half, 1)
                if not isinstance(r, int):
                    dve.wait_ge(idx_cp, E * r)
                dve.wait_ge(idx_half, r + 1)
                dve.tensor_tensor(idx_all[:, :], idx_rows[:, :], bank[4][0:CAP, E:2 * E], ALU.add).then_inc(idx_ok, 1)

            token_slots()
            link(dve.tensor_reduce(cnt[:, :], bank[7][:, NT * E:NT * E + E], AX.X, ALU.max))
            dve.tensor_scalar(flag[:, :], cnt[:, :], CAP + 0.5, None, ALU.is_gt).then_inc(flag_ok, 1)
            slot_tokens(0)
            dve.wait_ge(r_exp, 2)
            link(dve.tensor_reduce(r1[6][:, :], r4[1][:, :, :], AX.X, ALU.add))
            link(dve.tensor_scalar(r1[7][:, :], r1[5][:, :], 1.0, None, ALU.add))
            link(dve.tensor_tensor(r1[8][:, :], r1[6][:, :], r1[7][:, :], ALU.mult))
            link(dve.reciprocal(gate[0][:, :], r1[8][:, :]))
            dve.tensor_tensor(gate[1][:, :], gate[0][:, :], r1[5][:, :], ALU.mult)
            ids = iota_e[:, :].rearrange("p (a e) -> p a e", a=1).broadcast_to([P, NT, E])
            for c in range(2):
                rk, eid, rd = r1[6 + c], r1[8 + c], r1[10 + c]
                link(dve.tensor_tensor(s16, s2[c], ids, ALU.mult))
                link(dve.tensor_reduce(eid[:, :], s16, AX.X, ALU.add))
                link(dve.tensor_scalar(rd[:, :], rank_of[c][:, :], float(CAP), None, ALU.is_ge))
                for j in range(2, ROUNDS):
                    link(dve.scalar_tensor_tensor(out=rd[:, :], in0=rank_of[c][:, :], scalar=float(j * CAP), in1=rd[:, :],
                                                  op0=ALU.is_ge, op1=ALU.add))
                link(dve.scalar_tensor_tensor(out=rk[:, :], in0=rd[:, :], scalar=-float(CAP), in1=rank_of[c][:, :], op0=ALU.mult,
                                              op1=ALU.add))
                link(dve.scalar_tensor_tensor(out=rk[:, :], in0=eid[:, :], scalar=float(CAP), in1=rk[:, :], op0=ALU.mult, op1=ALU.add))
                ins = dve.scalar_tensor_tensor(out=pos_y[c][:, :], in0=rd[:, :], scalar=float(SLOTS), in1=rk[:, :], op0=ALU.mult,
                                               op1=ALU.add)
            ins.then_inc(places_ok, 1)

            def moe(r):
                s0, u0 = E * r, 3 * E * r

                def lo(m3, slot, unit, n=UNIT):
                    dve.wait_ge(m_hi, unit + 1)
                    dve.tensor_tensor(wlo[SPLIT_OF[m3]][:, 0:n], eraw[slot][:, 0:n], whi[SPLIT_OF[m3]][:, 0:n].bitcast(F32),
                                      ALU.subtract).then_inc(m_lo, 1)

                def tokens_lo(i, p):
                    for b in range(2):
                        dve.wait_ge(xsT_hi_ok, 2 * (s0 + i) + b + 1)
                        dve.tensor_tensor(xsT_lo[p][:, 4 * b:4 * b + 4, :].rearrange("p k n -> p (k n)"), bank[5 + b][:, 0:4 * CAP],
                                          xsT_hi[p][:, 4 * b:4 * b + 4, :].rearrange("p k n -> p (k n)").bitcast(F32),
                                          ALU.subtract).then_inc(xsT_lo_ok, 1)

                def times_up(i, p):
                    dve.wait_ge(silu_ok, s0 + i + 1)
                    dve.tensor_tensor(sg[p][:, :], sg[p][:, :], bank[p][0:CAP, FF:CB], ALU.mult).then_inc(a_ok, 1)

                def act_lo(i, p):
                    dve.wait_ge(aT_hi_ok, s0 + i + 1)
                    dve.tensor_tensor(aT_lo[p][:, :, :].rearrange("p k n -> p (k n)"), bank[7][:, 0:2 * CAP],
                                      aT_hi[p][:, :, :].rearrange("p k n -> p (k n)").bitcast(F32), ALU.subtract)\
                       .then_inc(aT_lo_ok, 1)

                def out_rows(i, p, n):
                    dve.wait_ge(m_used, u0 + down_used(i))
                    if not (isinstance(r, int) and isinstance(i, int) and i < 2):
                        dve.wait_ge(y_st[p], 16 * ((E // 2) * r + n))
                    dve.tensor_copy(yout[p][:, CB:D], bank[3][0:CAP, :]).then_inc(y_dve, 1)

                def step(i, j, a):
                    first = isinstance(i, int) and i == 0
                    last = isinstance(i, int) and i == E - 1
                    p = i % 2 if isinstance(i, int) else (3 + a) % 2
                    if not first:
                        lo(1, unit_at(i, 2, j, a)[0], u0 + 3 * i + 1, UNIT // 2)
                        act_lo(i - 1, 1 - p)
                    if not first:
                        lo(2, unit_at(i, 3, j, a)[0], u0 + 3 * i + 2, UNIT // 2 if last else UNIT)
                    if first:
                        lo(0, unit_at(i, 4, j, a)[0], u0 + 3)
                    if not last:
                        tokens_lo(i + 1, 1 - p)
                    times_up(i, p)
                    if not first and not last:
                        lo(0, unit_at(i, 4, j, a)[0], u0 + 3 * i + 3)
                    if not first:
                        out_rows(i - 1, 1 - p, half_of(i - 1, j, 2 + a))

                if not isinstance(r, int):
                    for c in range(2):
                        ins = dve.tensor_scalar(rank_of[c][:, :], rank_of[c][:, :], -float(CAP), None, ALU.add)
                    ins.then_inc(rank_less, 1)
                    dve.wait_ge(rank_less, r)
                    token_slots()
                    slot_tokens(r)
                dve.wait_ge(m_lo, u0 + 3)
                tokens_lo(0, 0)
                for i in range(3):
                    step(i, 0, 0)
                with dve.Fori(0, (E - 4) // BODY) as j:
                    for a in range(BODY):
                        step(BODY * j + 3 + a, j, a)
                step(E - 1, 0, 0)
                act_lo(E - 1, 1)
                out_rows(E - 1, 1, E // 2 - 1)

            moe(0)
            more = dve.value_load(flag[0:1, 0:1], min_val=0, max_val=1)
            with dve.If(more != 0):
                with dve.Fori(1, ROUNDS) as r:
                    moe(r)

            for t in range(NT):
                p = rows[t]
                dve.wait_ge(yg_ld[t], 32)
                for c in range(2):
                    ins = dve.scalar_tensor_tensor(out=x_sb[0:p, t, :], in0=yg[c][t][0:p, :], scalar=gate[c][0:p, t:t + 1],
                                                   in1=x_sb[0:p, t, :], op0=ALU.mult, op1=ALU.add)
                    if c == 0:
                        link(ins)
                ins.then_inc(y_ok, 1)

        @block.tensor
        def _(pe):
            pe.wait_ge(pc, PC_IDENT)

            def turn4(dst, src, n, done):
                for k in range(4):
                    mm = pe.transpose(dst[:, k * P:k * P + n], src[0:n, k * P:(k + 1) * P], ident[0:n, 0:n])
                mm.then_inc(done, 1)

            def turn_x(t):
                pe.wait_ge(xn_ok, t + 1)
                for b in range(2):
                    wait_turn(pe, X_USE + 2 * t + b)
                    turn4(turn_bank(X_USE + 2 * t + b), xn[t % 2][:, 4 * b * P:(4 * b + 4) * P], rows[t], x_tr)

            def next_x(t):
                if t + 2 < NT:
                    turn_x(t + 2)
                elif t + 2 == NT:
                    pe.wait_ge(ws_masked, 1)
                    for g in range(GROUPS):
                        mm = pe.transpose(bank[7][:, g * P:(g + 1) * P], ws[:, g, :], ident[:, :])
                    mm.then_inc(ws_tr, 1)

            turn_x(0)
            turn_x(1)

            def three_passes(acc, x_hi, x_lo, w_hi, w_lo, start, stop):
                pe.matmul(acc, x_hi, w_hi, start=start, stop=False)
                pe.matmul(acc, x_hi, w_lo, start=False, stop=False)
                return pe.matmul(acc, x_lo, w_hi, start=False, stop=stop)

            def project(blk, after):
                for half in range(2):
                    n = 2 * blk + half
                    pe.wait_ge(hi_ok, n + 1)
                    pe.wait_ge(lo_ok, n + 1)
                    if blk == NB and half == 1:
                        pe.wait_ge(sbT_lo, NV)
                    for t in range(NT):
                        if blk == 0 and half == 0:
                            pe.wait_ge(xT_lo_ok, 2 * t + 2)
                        if blk >= 1 and half == 0:
                            bank_read(blk - 1, t)
                        for k in range(UK):
                            c = slice(k * CB, (k + 1) * CB)
                            kk = UK * half + k
                            if t == NT - 1:
                                for j in range(CB // P):
                                    mm = pe.matmul(bank[t][j * DEC:(j + 1) * DEC, 0:P], xT_s[:, kk, :],
                                                   raw[n % 3][:, c.start + j * P:c.start + (j + 1) * P],
                                                   start=(kk == 0), stop=(kk == KC - 1))
                                continue
                            mm = three_passes(bank[t][0:rows[t], :], xT_hi[:, kk, tok(t)], xT_lo[:, kk, tok(t)],
                                              whi[n % 2][:, c], wlo[n % 2][:, c], kk == 0, kk == KC - 1)
                        if half == 1:
                            mm.then_inc(proj_done, 1)
                        elif t == NT - 1:
                            mm.then_inc(half_done, 1)
                        if after[half]:
                            after[half](t)

            def bank_read(blk, t):
                name = BLOCKS[blk] if blk < NB else "out"
                if name == "gv":
                    pe.wait_ge(gv_gelu, t + 1)
                elif name == "u":
                    pe.wait_ge(acc_free[t], 1)
                elif name in ("q", "k"):
                    pe.wait_ge(qk_scaled, NT * (blk - 2) + t + 1)
                elif name == "v":
                    pe.wait_ge(v_ok, t + 1)
                else:
                    pe.wait_ge(acc_free[t], 2)

            def mix_rows(t):
                p = rows[t]
                pe.wait_ge(gvn_ok, t + 1)
                if t == 0:
                    pe.wait_ge(wmT_ok, 1)
                else:
                    pe.wait_ge(gm_ok, t)
                for g in range(GROUPS):
                    c = slice(g * P, (g + 1) * P)
                    mm = pe.matmul(bank[7][0:p, c], WmT[0:p, g, 0:p], gvn[0:p, t, c], start=True, stop=True)
                mm.then_inc(mixed, 1)

            def turn_qk(m):
                t = m % NT
                pe.wait_ge(qk_ok, m + 1)
                wait_turn(pe, QK_USE + m)
                turn4(turn_bank(QK_USE + m), qn[m % 2], rows[t], qk_tr)

            def turn_cache():
                for c in range(NCH):
                    pe.wait_ge(ld_ck[c // 2], 16)
                    wait_turn(pe, CK_USE + c)
                    turn4(turn_bank(CK_USE + c), xn[c // 2][:, (c % 2) * CB:(c % 2 + 1) * CB], P, ck_tr)

            def scores(h):
                z = z_of(h)
                if h == 0:
                    pe.wait_ge(qkT_ok, 2 * NT)
                    pe.wait_ge(pc, PC_MASK)
                    pe.wait_ge(gm_ok, NT)
                elif h == 1:
                    bank_read(NB - 1, 2)
                else:
                    pe.wait_ge(w_ok, 2 * (h - 2) + 1)
                    if h == 2:
                        pe.wait_ge(gmT_lo, NT)
                if h:
                    for bk, c0, n, c, q0 in regions:
                        if h >= 2 and c == 1:
                            pe.wait_ge(w_ok, 2 * (h - 2) + 2)
                        pe.matmul(z[bk][:, c0:c0 + n], kT[:, (h - 1) // 2, c * P:(c + 1) * P], qpad[:, h - 1, q0:SEQ],
                                  start=(c0 == 0), stop=True, skip_group_check=True)
                        mm = pe.matmul(z[bk][:, c0:c0 + P], identb[:, :], maskneg[:, :], start=False, stop=True,
                                       skip_group_check=True)
                        if bk == 0:
                            mm.then_inc(z_ok, 1)
                else:
                    pe.wait_ge(ckT_ok, NCH)
                    for bk, c0, n, c in s_regions:
                        kt, p = (ckT[:, :, c * P:(c + 1) * P], P) if c < NCH else (kT[:, :, SEQ:TOK], DEC)
                        for j in range(KCH):
                            w0 = c0 + j // 2 * P
                            mm = pe.matmul(z[bk][0:p, w0:w0 + P], kt[:, j, :], qs[:, j * P:(j + 1) * P],
                                           start=(c0 == 0 and j == 0), stop=True, skip_group_check=True)
                        if c == 1:
                            mm.then_inc(z_ok, 1)
                    mm = pe.matmul(z[bk][0:DEC, c0:c0 + n], identb[0:DEC, 0:DEC], maskneg8[:, :, :].rearrange("p h n -> p (h n)"),
                                   start=False, stop=True, skip_group_check=True)
                mm.then_inc(z_ok, 1)

            def suffix_sums(h):
                z, s = z_of(h), sp[h % 2]
                pe.wait_ge(sp_ok, h + 1)
                pe.wait_ge(pc, PC_U)
                u = later_sums(h)
                for bk, c0, n, c, *_ in (regions if h else s_regions):
                    p = P if h or c < NCH else DEC
                    pe.matmul(z[bk][0:p, c0:c0 + n], negU[0:p, 0:p], s[0:p, 512 * bk + c0:512 * bk + c0 + n],
                              start=False, stop=True, skip_group_check=True)
                pe.wait_ge(later_ok, h + 1)
                if h:
                    rest = ((0, P, s[:, 512:512 + P]), (0, 2 * P, u[:, 0:2 * P]), (1, P, s[:, 1024:1024 + P]),
                            (1, 2 * P, u[:, 2 * P:3 * P]), (2, P, s[:, 896:1024]))
                else:
                    rest = ((0, 0, u[:, 0:DW]), (0, DW, u[:, DW:2 * DW]), (1, 0, u[:, 2 * DW:3 * DW]),
                            (1, DW, s[:, 1024:1024 + DW]))
                for k, (bk, c0, a) in enumerate(rest):
                    mm = pe.matmul(z[bk][:, c0:c0 + a.shape[-1]], negones[:, :], a, start=False, stop=True,
                                   skip_group_check=True)
                    if k == 1:
                        mm.then_inc(rest_ok, 1)
                mm.then_inc(rest_ok, 1)

            def values(v, chunks):
                o = bank[5 + v % 2]
                pe.wait_ge(w_ok, 2 * (2 * v + 1))
                if v >= 2:
                    pe.wait_ge(sbT_lo, v - 1)
                if v:
                    pe.wait_ge(v_ok, NT)
                    for bk, c0, n, c, q0 in sorted(regions, key=lambda x: x[3]):
                        if c not in chunks:
                            continue
                        for a in range(2):
                            h = 2 * v - 1 + a
                            mm = pe.matmul(o[a * HD:(a + 1) * HD, q0:SEQ], v_sb[:, c, (h - 1) * HD:h * HD],
                                           lw[h % 5][:, 512 * bk + c0:512 * bk + c0 + n],
                                           start=(c == 0), stop=True, skip_group_check=True)
                else:
                    pe.wait_ge(ld_cv, 16)
                    pe.wait_ge(v_ok, NT)
                    for j in range(KCH):
                        hc = slice(j * P, (j + 1) * P)
                        for bk, c0, n, c in s_regions:
                            vv, p = (cv[:, c, hc], P) if c < NCH else (v_sb[0:DEC, NT - 1, hc], DEC)
                            w0 = 512 * bk + c0 + j // 2 * P
                            mm = pe.matmul(o[:, hc], vv, lw[0][0:p, w0:w0 + P], start=(j == 0 and c == 0), stop=True,
                                           skip_group_check=True)
                if 1 in chunks:
                    mm.then_inc(pv_ok, 1)

            project(0, (next_x, None))
            turn_cache()
            project(1, (None, mix_rows))
            project(2, (None, None))
            project(3, (lambda t: turn_qk(t), None))
            project(4, (lambda t: turn_qk(NT + t), lambda t: scores(0) if t == 0 else None))

            scores(1)
            for t in range(NT):
                pe.wait_ge(gm_ok, t + 1)
                if t < 2:
                    bank_read(NB - 1, 3 + t)
                else:
                    pe.wait_ge(gmT_lo, t - 1)
                turn4(bank[3 + t % 2], gvn[:, t, :], rows[t], gm_tr)
            for h in range(NH):
                if h >= 4:
                    values(*((h // 2 - 1, (0, 3)) if h % 2 == 0 else (h // 2 - 1, (1, 2))))
                if 1 <= h < NH - 1:
                    scores(h + 1)
                suffix_sums(h)
                if h == 1:
                    values(0, (0, 1, 2, 3))
            values(NV - 2, (1, 2))
            values(NV - 1, (0, 1, 2, 3))

            pe.wait_ge(w_ok, 2 * NH)
            pe.wait_ge(gmT_lo, NT)
            project(NB, (None, None))

            def router(t):
                pe.wait_ge(x2T_ok, 2 * t + 2)
                if t == 0:
                    pe.wait_ge(wr_padded, 1)
                else:
                    pe.wait_ge(lg_ok, t)
                for k in range(KC):
                    mm = pe.matmul(bank[7][0:rows[t], 0:P], x2T_of[t][:, k, 0:rows[t]], wr_pad[:, k, :], start=(k == 0), stop=(k == KC - 1))
                mm.then_inc(r_mm, 1)

            def turn_normed(t):
                pe.wait_ge(xn2_ok, t + 1)
                for b in range(2):
                    if t >= 1:
                        pe.wait_ge(x2T_ok, 2 * t - 1 + b)
                    turn4(bank[5 + b], xn2_of[t][:, 4 * b * P:(4 * b + 4) * P], rows[t], x2_tr)

            def between(t):
                if t == 2:
                    turn_normed(0)
                elif t >= 3:
                    router(t - 3)
                    turn_normed(t - 2)

            project(NB + 1, (None, between))
            router(NT - 3)
            turn_normed(NT - 2)
            turn_normed(NT - 1)
            router(NT - 2)
            router(NT - 1)
            pe.wait_ge(selb_ok, 1)
            pe.wait_ge(lg_ok, NT)
            for t in range(NT):
                dst = bank[7][:, t * E:(t + 1) * E]
                for t2 in range(t):
                    pe.matmul(dst, onesb[:, :], selb[:, t2, :], start=(t2 == 0), stop=False)
                pe.matmul(dst, before[:, :], selb[:, t, :], start=(t == 0), stop=True)
            for t in range(NT):
                mm = pe.matmul(bank[7][:, NT * E:(NT + 1) * E], onesb[:, :], selb[:, t, :], start=(t == 0), stop=(t == NT - 1))
            mm.then_inc(rank_ok, 1)

            def slot_table(r):
                pe.wait_ge(onehot_ok, r + 1)
                for m in range(2 * NT):
                    mm = pe.matmul(bank[4][0:CAP, 0:2 * E], onehot[:, m, :], ids_of[:, m, :], start=(m == 0), stop=(m == 2 * NT - 1))
                mm.then_inc(ids_mm, 1)

            def moe(r):
                s0, u0 = E * r, 3 * E * r
                slot_table(r)

                def turn_tokens(i, p, n):
                    s = s0 + i
                    pe.wait_ge(xs_ld[p], 16 * ((E // 2) * r + n + 1))
                    for b in range(2):
                        if not (isinstance(s, int) and s < 1):
                            pe.wait_ge(xsT_lo_ok, 2 * s - 1 + b)
                        for k in range(4):
                            mm = pe.transpose(bank[5 + b][:, k * CAP:(k + 1) * CAP],
                                              xs[p][:, (4 * b + k) * P:(4 * b + k + 1) * P], ident[0:CAP, 0:CAP])
                        mm.then_inc(xs_tr, 1)

                def gate_up(i, p, half, m3, unit):
                    s = s0 + i
                    if half == 0:
                        pe.wait_ge(xsT_lo_ok, 2 * s + 2)
                        if isinstance(s, int) and s < 2:
                            pe.wait_ge(acc_free[s], 3)
                        else:
                            pe.wait_ge(a_ok, s - 1)
                    pe.wait_ge(m_lo, unit + 1)
                    for k in range(UK):
                        c = slice(k * CB, (k + 1) * CB)
                        kk = UK * half + k
                        mm = three_passes(bank[p][0:CAP, :], xsT_hi[p][:, kk, :], xsT_lo[p][:, kk, :],
                                          whi[SPLIT_OF[m3]][:, c], wlo[SPLIT_OF[m3]][:, c], kk == 0, kk == KC - 1)
                    mm.then_inc(m_used, 1)

                def turn_act(i, p):
                    s = s0 + i
                    pe.wait_ge(a_ok, s + 1)
                    if not (isinstance(s, int) and s < 1):
                        pe.wait_ge(aT_lo_ok, s)
                    for k in range(2):
                        mm = pe.transpose(bank[7][:, k * CAP:(k + 1) * CAP], sg[p][:, k * P:(k + 1) * P], ident[0:CAP, 0:CAP])
                    mm.then_inc(a_tr, 1)

                def down(i, p, m3, unit):
                    s = s0 + i
                    pe.wait_ge(aT_lo_ok, s + 1)
                    pe.wait_ge(m_lo, unit + 1)
                    pe.wait_ge(m_lo_pool, (E + 1) * r + i + 2)
                    if isinstance(s, int) and s < 1:
                        pe.wait_ge(acc_free[2], 3)
                        pe.wait_ge(acc_free[3], 3)
                    else:
                        pe.wait_ge(y_act, s)
                        pe.wait_ge(y_dve, s)
                    for n in range(2):
                        for k in range(2):
                            c = slice(k * D + n * CB, k * D + (n + 1) * CB)
                            mm = three_passes(bank[2 + n][0:CAP, :], aT_hi[p][:, k, :], aT_lo[p][:, k, :],
                                              whi[SPLIT_OF[m3]][:, c], wlo[SPLIT_OF[m3]][:, c], k == 0, k == 1)
                    mm.then_inc(m_used, 1)

                def step(i, j, a):
                    p = i % 2 if isinstance(i, int) else (3 + a) % 2
                    first = isinstance(i, int) and i == 0
                    last = isinstance(i, int) and i == E - 1
                    gate_up(i, p, 0, 0 if first else 2, u0 + (0 if first else 3 * i - 1))
                    if first:
                        turn_tokens(1, 1, 0)
                    else:
                        turn_act(i - 1, 1 - p)
                    gate_up(i, p, 1, 1 if first else 0, u0 + (1 if first else 3 * i))
                    if not first and not last:
                        turn_tokens(i + 1, 1 - p, half_of(i + 1, j, 4 + a))
                    if not first:
                        down(i - 1, 1 - p, 1, u0 + 3 * i + 1)

                turn_tokens(0, 0, 0)
                for i in range(3):
                    step(i, 0, 0)
                with pe.Fori(0, (E - 4) // BODY) as j:
                    for a in range(BODY):
                        step(BODY * j + 3 + a, j, a)
                step(E - 1, 0, 0)
                turn_act(E - 1, 1)
                down(E - 1, 1, 2, u0 + 3 * E - 1)

            moe(0)
            pe.wait_ge(flag_ok, 1)
            more = pe.value_load(flag[0:1, 0:1], min_val=0, max_val=1)
            with pe.If(more != 0):
                with pe.Fori(1, ROUNDS) as r:
                    moe(r)


_INS = ["x_prompt", "x_sample", "cache_sb_k", "cache_sb_v", "norm1_g", "w_in", "gm_v_norm_g", "gm_w_s", "gm_b_s",
        "q_norm_g", "k_norm_g", "w_out", "norm2_g", "w_router_group", "b_router_group", "w_router_expert",
        "b_router_expert", "w_gate", "w_up", "w_down"]


def kernel(**inputs):
    import numpy as _np
    import concourse.bacc as _bacc
    from concourse import mybir as _mybir
    from concourse.bass_utils import run_bass_kernel_spmd as _run

    nc = _bacc.Bacc("TRN2", target_bir_lowering=False, num_devices=1)
    arrays, args = {}, []
    for name in _INS:
        a = _np.ascontiguousarray(inputs[name])
        arrays[f"in_{name}_dram"] = a
        args.append(nc.dram_tensor(f"in_{name}_dram", a.shape, _mybir.dt.from_np(a.dtype), kind="ExternalInput").ap())
    xp, xs, ck = inputs["x_prompt"].shape, inputs["x_sample"].shape, inputs["cache_sb_k"].shape
    groups = inputs["gm_w_s"].shape[1]
    outs = [xp, xs] + [(1, *xp[:2], *ck[3:])] * 2 + [(1, *xs[:2], *ck[3:])] * 2
    outs.append((1, *xs[:2], groups, inputs["gm_v_norm_g"].shape[1] // groups))
    for i, shape in enumerate(outs):
        args.append(nc.dram_tensor(f"out_{i}_dram", shape, _mybir.dt.float32, kind="ExternalOutput").ap())
    trunk_step(nc, *args)
    r = _run(nc, [arrays], core_ids=[0])
    return tuple(r.results[0][f"out_{i}_dram"] for i in range(len(outs)))
```
